# Optimizing a Trainium2 kernel written in Bass

```python
import jax, jax.numpy as jnp
from jax import lax
import numpy as np

D_MODEL = 1024
BATCH = 1
SEQ = 2048
DEPTH = 1
DEC_BATCH = 1
DEC_SEQ = 512
PAST_LEN = 128

N_META = 16
EPS = 1e-6
CONV_WIDTH = 3 * D_MODEL // 8
CONV_HEADS = 6
POOL_GROUPS = 4
POOL_WINDOWS = (2, 4, 8, 16)
POOL_WIDTH = 3 * D_MODEL // 8
POOL_GROUP_DIM = POOL_WIDTH // POOL_GROUPS
FOURIER_HEADS = 4
FOURIER_WIDTH = D_MODEL - CONV_WIDTH - POOL_WIDTH
FOURIER_HEAD_DIM = FOURIER_WIDTH // FOURIER_HEADS
MIX_WIDTH = CONV_WIDTH + POOL_WIDTH + FOURIER_WIDTH
IN_WIDTH = 3 * CONV_WIDTH + POOL_WIDTH + FOURIER_WIDTH
D_FF = -(-8 * D_MODEL // (3 * 256)) * 256

kernel_name = "hymba_conv_pool_fourier_encoder"

def _rms(x):
    xf = x.astype(jnp.float32)
    return xf * lax.rsqrt(jnp.mean(xf * xf, axis=-1, keepdims=True) + EPS)

def _rmsnorm(x, g):
    return (_rms(x) * g.astype(jnp.float32)).astype(x.dtype)

def _short_conv(u, w):
    up = jnp.pad(u, ((0, 0), (1, 1), (0, 0)))
    return up[:, :-2] * w[0] + up[:, 1:-1] * w[1] + up[:, 2:] * w[2]

def _centred_mean_minus_self(u, window):
    L = u.shape[1]
    left = window // 2
    right = window - 1 - left
    uf = u.astype(jnp.float32)
    cs = jnp.pad(jnp.cumsum(uf, axis=1), ((0, 0), (1, 0), (0, 0)))
    csp = jnp.pad(cs, ((0, 0), (left, right), (0, 0)), mode="edge")
    hi = csp[:, left + right + 1:left + right + 1 + L]
    lo = csp[:, :L]
    pos = jnp.arange(L)
    cnt = (jnp.minimum(pos + right, L - 1) - jnp.maximum(pos - left, 0) + 1).astype(jnp.float32)
    return ((hi - lo) / cnt[None, :, None] - uf).astype(u.dtype)

def _multiscale_pool(u, pool_w, pool_scale):
    outs = []
    for gi, win in enumerate(POOL_WINDOWS):
        ug = u[..., gi * POOL_GROUP_DIM:(gi + 1) * POOL_GROUP_DIM]
        outs.append(_centred_mean_minus_self(ug, win) @ pool_w[gi])
    return jnp.concatenate(outs, axis=-1) * pool_scale

def _fourier(u):
    B_, L, _ = u.shape
    uh = u.astype(jnp.float32).reshape(B_, L, FOURIER_HEADS, FOURIER_HEAD_DIM).transpose(0, 2, 1, 3)
    f = jnp.fft.fft2(uh, axes=(-2, -1), norm="ortho").real
    return f.transpose(0, 2, 1, 3).reshape(B_, L, FOURIER_WIDTH).astype(u.dtype)

def _layer(h, norm1_g, w_in, conv_w, pool_w, pool_scale, mix_g, w_out, norm2_g, w_gate_up, w_down):
    u = _rmsnorm(h, norm1_g)
    z = u @ w_in
    c0 = CONV_WIDTH
    xa, gb, gc = z[..., :c0], z[..., c0:2 * c0], z[..., 2 * c0:3 * c0]
    xp = z[..., 3 * c0:3 * c0 + POOL_WIDTH]
    xf = z[..., 3 * c0 + POOL_WIDTH:]
    a = gb * _short_conv(gc * xa, conv_w)
    p = _multiscale_pool(xp, pool_w, pool_scale)
    f = _fourier(xf)
    mix = jnp.concatenate([_rms(a), _rms(p), _rms(f)], axis=-1) * mix_g.astype(jnp.float32)
    h = h + mix.astype(h.dtype) @ w_out
    v = _rmsnorm(h, norm2_g)
    gu = v @ w_gate_up
    gate, up = gu[..., :D_FF], gu[..., D_FF:]
    return h + (jax.nn.silu(gate) * up) @ w_down

def _trunk(x, meta_tokens, norm1_g, w_in, conv_w, pool_w, pool_scale, mix_g, w_out, norm2_g, w_gate_up, w_down, final_g):
    B_ = x.shape[0]
    meta = jnp.broadcast_to(meta_tokens.astype(x.dtype)[None], (B_, N_META, D_MODEL))
    h = jnp.concatenate([meta, x], axis=1)
    for l in range(DEPTH):
        h = _layer(h, norm1_g[l], w_in[l], conv_w[l], pool_w[l], pool_scale[l], mix_g[l],
                   w_out[l], norm2_g[l], w_gate_up[l], w_down[l])
    return _rmsnorm(h, final_g)[:, N_META:]

def setup_inputs(seed: int = 0) -> dict:
    key = jax.random.key(seed)
    ks = jax.random.split(key, 16)
    f32 = jnp.float32
    nrm = lambda k, shape, s: jax.random.normal(k, shape, f32) * s
    return {
        "x_prompt": nrm(ks[0], (BATCH, SEQ, D_MODEL), 1.0),
        "x_sample": nrm(ks[1], (DEC_BATCH, DEC_SEQ, D_MODEL), 1.0),
        "meta_tokens": nrm(ks[2], (N_META, D_MODEL), 1.0),
        "norm1_g": 1.0 + nrm(ks[3], (DEPTH, D_MODEL), 0.02),
        "w_in": nrm(ks[4], (DEPTH, D_MODEL, IN_WIDTH), D_MODEL ** -0.5),
        "conv_w": nrm(ks[5], (DEPTH, 3, CONV_WIDTH), 3 ** -0.5),
        "pool_w": nrm(ks[6], (DEPTH, POOL_GROUPS, POOL_GROUP_DIM, POOL_GROUP_DIM), POOL_GROUP_DIM ** -0.5),
        "pool_scale": 1.0 + nrm(ks[7], (DEPTH, POOL_WIDTH), 0.1),
        "mix_g": 1.0 + nrm(ks[8], (DEPTH, MIX_WIDTH), 0.02),
        "w_out": nrm(ks[9], (DEPTH, MIX_WIDTH, D_MODEL), MIX_WIDTH ** -0.5),
        "norm2_g": 1.0 + nrm(ks[10], (DEPTH, D_MODEL), 0.02),
        "w_gate_up": nrm(ks[11], (DEPTH, D_MODEL, 2 * D_FF), D_MODEL ** -0.5),
        "w_down": nrm(ks[12], (DEPTH, D_FF, D_MODEL), D_FF ** -0.5),
        "final_g": 1.0 + nrm(ks[13], (D_MODEL,), 0.02),
    }

def reference(x_prompt, x_sample, meta_tokens, norm1_g, w_in, conv_w, pool_w, pool_scale, mix_g,
              w_out, norm2_g, w_gate_up, w_down, final_g):
    y_prompt = _trunk(x_prompt, meta_tokens, norm1_g, w_in, conv_w, pool_w, pool_scale, mix_g,
                      w_out, norm2_g, w_gate_up, w_down, final_g)
    y_sample = _trunk(x_sample, meta_tokens, norm1_g, w_in, conv_w, pool_w, pool_scale, mix_g,
                      w_out, norm2_g, w_gate_up, w_down, final_g)
    return (y_prompt, y_sample)


_drawn_inputs = setup_inputs


def setup_inputs(seed=0):
    import zlib

    import numpy as np

    out = dict(_drawn_inputs(seed))
    spreads = {}
    factors = {'norm1_g': 2.941, 'mix_g': 3.879, 'norm2_g': 5.215, 'final_g': 2.739}
    for name, (base, spread) in spreads.items():
        noise = np.random.default_rng([zlib.crc32(name.encode()), seed]).standard_normal(out[name].shape)
        drawn = base * np.exp(spread * noise) if base else spread * noise
        out[name] = __import__('jax').numpy.asarray(drawn.astype(out[name].dtype))
    for name, factor in factors.items():
        out[name] = (out[name] * factor).astype(out[name].dtype)
    return out
```

```python
from contextlib import ExitStack

import numpy as np

import concourse.bass as bass
from concourse import mybir
from concourse.alu_op_type import AluOpType as ALU

ACT = mybir.ActivationFunctionType
F32 = mybir.dt.float32
F32R = mybir.dt.float32r

P = 128
D = 1024
KD = D // P
META = 16
SEQ, DEC = 2048, 512
L1, L2 = META + SEQ, META + DEC
T = 512
NT = T // P
NB1 = SEQ // T
NBLK = (SEQ + DEC) // T
CONV = 3 * D // 8
GROUP = CONV // 4
FOUR = D - 2 * CONV
HD = FOUR // 4
DFF = -(-8 * D // (3 * 256)) * 256
MF = DFF // P
EPS = 1e-6
NPAN = 3 * CONV // P
KCH = 344
NCH = 3
K2 = L2 // 2
WINDOWS = (2, 4, 8, 16)
UNITS = 4 + MF + MF // 2
assert NCH * KCH == L1 // 2 and DFF % 256 == 0 and UNITS % 2 == 1


def split_product(pe, out, w, x, first, last):
    pe.matmul(out, w[0], x[0], start=first, stop=False, skip_group_check=True)
    pe.matmul(out, w[0], x[1], start=False, stop=False, skip_group_check=True)
    return pe.matmul(out, w[1], x[0], start=False, stop=last, skip_group_check=True)


class Chain:

    def __init__(self, eng, sem, base=0):
        self.eng, self.sem, self.base, self.n = eng, sem, base, 0

    def step(self, ins):
        self.n += 1
        ins.then_inc(self.sem, 1)
        self.eng.wait_ge(self.sem, self.base + self.n)


def prepare(nc, c, w_hi, w_lo):
    RAW = 3
    with ExitStack() as ctx:
        sb = lambda n, s, d=F32: ctx.enter_context(nc.sbuf_tensor(n + "_sb", s, d))
        sem = lambda n: ctx.enter_context(nc.semaphore(n))
        raw = sb("raw_panel", [P, RAW, D])
        wp = sb("w_pool_T", [GROUP, 4, D])
        pw = sb("pool_w", [GROUP, 4, GROUP])
        bank = ctx.enter_context(nc.psum_tensor("fold_bank", [P, 8, 512], F32))
        raw_landed = [sem(f"raw_landed{i}") for i in range(RAW)]
        wp_landed = sem("wp_landed")
        hi_made, lo_made = sem("hi_made"), sem("lo_made")
        fold_done, fold_hi = sem("fold_done"), sem("fold_hi")
        panels = [j for j in range(NPAN)] + [NPAN + 3, NPAN + 4]
        block = ctx.enter_context(nc.Block())

        def folded(w, g, h):
            return w[:, NPAN:NPAN + 3, 4 * h:4 * h + 4, 32 * g:32 * g + 32]

        def fold_bank(g, h):
            return bank[:, 2 * g + h, 0:4 * GROUP].rearrange("p (k t j) -> p t k j", k=4, t=3)

        @block.sync
        def _(sp):
            sp.dma_start(wp[:, :, :], c["w_pool_T"].rearrange("g j k -> j g k")).then_inc(wp_landed, 16)
            sp.dma_start(pw[:, :, :], c["pool_w"].rearrange("g j o -> j g o")).then_inc(wp_landed, 16)
            for n, j in enumerate(panels):
                if n >= RAW:
                    sp.wait_ge(lo_made, n - RAW + 1)
                src = c["w_in_panels"][n, :, :]
                sp.dma_start(raw[:, n % RAW, :], src).then_inc(raw_landed[n % RAW], 16)

        @block.scalar
        def _(act):
            for n, j in enumerate(panels):
                act.wait_ge(raw_landed[n % RAW], 16 * (n // RAW + 1))
                act.activation(w_hi[:, j, :, :], raw[:, n % RAW, :].rearrange("p (k n) -> p k n", k=KD),
                               ACT.Copy).then_inc(hi_made, 1)
                if n == 5:
                    for g in range(4):
                        for h in range(2):
                            act.wait_ge(fold_done, 2 * g + h + 1)
                            for t in range(3):
                                ins = act.activation(folded(w_hi, g, h)[:, t], fold_bank(g, h)[:, t], ACT.Copy)
                            ins.then_inc(fold_hi, 1)

        @block.vector
        def _(dve):
            for n, j in enumerate(panels):
                dve.wait_ge(hi_made, n + 1)
                dve.tensor_tensor(w_lo[:, j, :, :], raw[:, n % RAW, :].rearrange("p (k n) -> p k n", k=KD),
                                  w_hi[:, j, :, :].bitcast(F32), ALU.subtract).then_inc(lo_made, 1)
                if n == 5:
                    for g in range(4):
                        for h in range(2):
                            dve.wait_ge(fold_hi, 2 * g + h + 1)
                            for t in range(3):
                                dve.tensor_tensor(folded(w_lo, g, h)[:, t], fold_bank(g, h)[:, t],
                                                  folded(w_hi, g, h)[:, t].bitcast(F32), ALU.subtract)

        @block.tensor
        def _(pe):
            pe.wait_ge(wp_landed, 32)
            for g in range(4):
                for h in range(2):
                    for k in range(4):
                        ins = pe.matmul(bank[:, 2 * g + h, k * GROUP:(k + 1) * GROUP],
                                        wp[:, g, (4 * h + k) * P:(4 * h + k + 1) * P], pw[:, g, :],
                                        start=True, stop=True)
                    ins.then_inc(fold_done, 1)


def project(nc, c, w_hi, w_lo, ident, half, ones, eps):
    HALO = 8
    W = META + T
    ROUNDS = NBLK + 1
    with ExitStack() as ctx:
        sb = lambda n, s, d=F32: ctx.enter_context(nc.sbuf_tensor(n + "_sb", s, d))
        sem = lambda n: ctx.enter_context(nc.semaphore(n))
        u_hi = sb("u_hi", [P, KD, T], F32R)
        u_lo = sb("u_lo", [P, KD, T], F32R)
        xt = sb("x_tiles", [P, NT, D])
        junk = sb("junk", [P, D])
        g1 = sb("norm1_rows", [P, D])
        msq = sb("mean_sq", [P, NT])
        ms = sb("mean_sq_eps", [P, NT])
        rstd = sb("rstd", [P, NT])
        xa = sb("xa", [P, T])
        gated = sb("gated", [P, 3, W])
        outer = sb("outer_gate", [P, 3, W])
        zp = sb("z_pool", [P, 3, W])
        meta3 = sb("meta3", [P, 3, 3, META])
        win = sb("window_sums", [P, 4, W])
        res = sb("mix_tiles", [P, 2, T])
        tail = sb("mix_tails", [P, 6, HALO])
        cw = sb("conv_w", [P, 3, 3])
        ps = sb("pool_scale", [P, 3])
        icnt = sb("inv_counts", [P, HALO])
        xf_st = sb("xf_stage", [P, 2, FOUR])
        bank = ctx.enter_context(nc.psum_tensor("proj_bank", [P, 8, 512], F32))

        consts = sem("consts_landed")
        landed = [sem(f"x_landed{i}") for i in range(NT)]
        squared, rstd_made, rstd_step, normed = sem("squared"), sem("rstd_made"), sem("rstd_step"), sem("normed")
        transposed, u_hi_made, u_lo_made = sem("transposed"), sem("u_hi_made"), sem("u_lo_made")
        panel_done, read_act, gated_made = sem("panel_done"), sem("read_act"), sem("gated_made")
        carried, step = sem("carried"), sem("vector_step")
        mix_made = sem("mix_made")
        mix_stored = [sem(f"mix_stored{i}") for i in range(2)]
        tail_made, tail_stored = sem("tail_made"), sem("tail_stored")
        xf_done, xf_read = sem("xf_done"), sem("xf_read")
        xf_stored = [sem(f"xf_stored{i}") for i in range(2)]
        block = ctx.enter_context(nc.Block())

        ORDER = [q for t in range(3) for q in (t, 6 + t, 3 + t)] + [NPAN + t for t in range(3)]
        READS = {0: "act", 1: "dve", 2: "act"}
        act_index = {}
        for i in range(12):
            if i >= 9 or i % 3 != 1:
                act_index[i] = len(act_index)

        def tile(r, t):
            return 4 * r - 3 + t if not isinstance(r, int) or r else 0

        def rounds(eng, body, flush=None):
            body(0, META, False)
            with eng.Fori(1, NB1 + 1) as r:
                body(r, T, True)
            if flush:
                flush(0)
            body(NB1 + 1, T, False)
            if flush:
                flush(1)

        @block.sync
        def _(sp):
            for dst, name in ((ident[:, :], "ident"), (g1[:, :], "norm1_rows"), (cw[:, :, :], "conv_cols"),
                              (ps[:, :], "pool_scale_cols"), (icnt[:, :], "inv_counts"),
                              (half[:, :], "minus_half"), (ones[:, :], "ones"), (eps[:, :], "eps")):
                sp.dma_start(dst, c[name]).then_inc(consts, 16)
            sp.dma_start(xt[0:META, 0, :], c["meta"]).then_inc(landed[0], 16)
            for s in (*mix_stored, *xf_stored):
                sp.nop().then_inc(s, 16)

            def load(r, t):
                if not (isinstance(r, int) and r == 0 and t):
                    sp.wait_ge(transposed, 2 * tile(r, t) + 2)
                row = T * r + P * t
                sp.dma_start(xt[:, t, :], c["x"][bass.ds(row, P), :]).then_inc(landed[t], 16)

            def body(r, n, more):
                if more or isinstance(r, int) and r == 0:
                    for t in range(NT):
                        load(r, t)
                is_meta = isinstance(r, int) and r == 0
                last = isinstance(r, int) and r
                if not is_meta:
                    col, skip = (META + SEQ, HALO) if last else (T * r - T + HALO, 0)
                    for i in range(6):
                        sp.wait_ge(mix_made, 6 * r - 6 + i + 1)
                        sp.dma_start(c["mixT"][P * i:P * i + P, bass.ds(col, T - skip)], res[:, i % 2, skip:T])\
                            .then_inc(mix_stored[i % 2], 16)
                for t in range(1 if is_meta else NT):
                    s = 1 if is_meta else t % 2
                    sp.wait_ge(xf_read, tile(r, t) + 2)
                    if is_meta:
                        sp.dma_start(c["xf"][NT * NBLK, 0:META, :], xf_st[0:META, s, :]).then_inc(xf_stored[s], 16)
                    else:
                        sp.dma_start(c["xf"][bass.ds(4 * r - 4 + t, 1), :, :].rearrange("a p n -> p (a n)"),
                                     xf_st[:, s, :]).then_inc(xf_stored[s], 16)

            def flush(q):
                sp.wait_ge(tail_made, q + 1)
                col = META + (SEQ, SEQ + DEC)[q] - HALO
                sp.dma_start(c["mixT"][0:6 * P, col:col + HALO].rearrange("(i p) n -> p i n", p=P),
                             tail[:, :, :]).then_inc(tail_stored, 16)

            rounds(sp, body, flush)
            sp.wait_ge(tail_stored, 32)
            for s in mix_stored:
                sp.wait_ge(s, 16 * (1 + 3 * NBLK))
            sp.wait_ge(xf_stored[0], 16 * (1 + 2 * NBLK))
            sp.wait_ge(xf_stored[1], 16 * (2 + 2 * NBLK))

        @block.gpsimd
        def _(pool):
            pool.wait_ge(consts, 16 * 8)

            def rms(n, rows, t):
                pool.wait_ge(squared, n + 1)
                pool.tensor_tensor(ms[0:rows, t:t + 1], msq[0:rows, t:t + 1], eps[0:rows, :], ALU.add)\
                    .then_inc(rstd_step, 1)
                pool.wait_ge(rstd_step, n + 1)
                pool.tensor_tensor(rstd[0:rows, t:t + 1], ms[0:rows, t:t + 1], half[0:rows, 0:1], ALU.pow)\
                    .then_inc(rstd_made, 1)

            rms(0, META, 0)
            with pool.Fori(1, NBLK + 1) as r:
                for t in range(NT):
                    rms(tile(r, t), P, t)

        @block.scalar
        def _(act):
            act.wait_ge(consts, 16 * 8)
            act.nop().then_inc(xf_read, 1)

            def square(r, t, rows=P):
                n = tile(r, t)
                act.wait_ge(landed[t], 16 * (r + (t == 0)) if not isinstance(r, int) or r else 16)
                if not isinstance(r, int) or r:
                    act.wait_ge(squared, n)
                act.activation(junk[0:rows, :], xt[0:rows, t, :], ACT.Square, scale=D ** -0.5,
                               accum_out=msq[0:rows, t:t + 1]).then_inc(squared, 1)

            def body(r, n, more):
                is_meta = isinstance(r, int) and r == 0
                last = isinstance(r, int) and r
                tiles, rows, off = (1, META, 0) if is_meta else (NT, P, META)
                more = more or is_meta
                for t in range(tiles):
                    for h in range(2):
                        act.wait_ge(transposed, 2 * tile(r, t) + h + 1)
                        act.activation(u_hi[:, 4 * h:4 * h + 4, P * t:P * t + rows],
                                       bank[:, 6 + h, :].rearrange("p (k n) -> p k n", k=4)[:, :, 0:rows],
                                       ACT.Copy).then_inc(u_hi_made, 1)
                for i in range(12):
                    q, t = i % 3, i // 3 if i < 9 else i - 9
                    if i < 9 and q == 1:
                        continue
                    act.wait_ge(panel_done, 12 * r + i + 1)
                    if i < 9 and q == 0:
                        dst = xa[:, 0:n]
                        if not (is_meta and t == 0):
                            act.wait_ge(gated_made, 3 * r + t)
                    elif i < 9:
                        dst = outer[:, t, off:off + n]
                        if not is_meta:
                            act.wait_ge(carried, 6 * r - 6 + t + 1)
                    else:
                        dst = zp[:, t, off:off + n]
                        if not is_meta:
                            act.wait_ge(carried, 6 * r - 6 + 3 + t + 1)
                    if last and i == 2:
                        act.wait_ge(tail_made, 1)
                    act.activation(dst, bank[:, i % 4, 0:n], ACT.Copy).then_inc(read_act, 1)
                    if more and i in (2, 5, 8, 9):
                        t2 = {2: 0, 5: 1, 8: 2, 9: 3}[i]
                        square(r + 1, t2)
                for t in range(tiles):
                    s = 1 if is_meta else t % 2
                    act.wait_ge(xf_done, tile(r, t) + 1)
                    if is_meta:
                        act.wait_ge(xf_stored[s], 16)
                    elif s == 0:
                        act.wait_ge(xf_stored[s], 16 * (2 * r - 2 + t // 2 + 1))
                    else:
                        act.wait_ge(xf_stored[s], 16 * (2 * r - 2 + t // 2 + 2))
                    act.activation(xf_st[0:rows, s, :], bank[0:rows, 4 + s, 0:FOUR], ACT.Copy).then_inc(xf_read, 1)

            square(0, 0, META)
            rounds(act, body)

        @block.vector
        def _(dve):
            dve.wait_ge(consts, 16 * 8)
            STEPS = 3 * 3 + 3 * 8
            TAIL_STEPS = 3 + 3 * 4 + 3 * 10 + 3

            def norm(r, t, rows=P):
                dve.wait_ge(rstd_made, tile(r, t) + 1)
                dve.scalar_tensor_tensor(out=xt[0:rows, t, :], in0=xt[0:rows, t, :], scalar=rstd[0:rows, t:t + 1],
                                         in1=g1[0:rows, :], op0=ALU.mult, op1=ALU.mult).then_inc(normed, 1)

            def conv(ch, t, dst, n, out_sem):
                g = lambda d: gated[:, t, HALO + d:HALO + d + n]
                ch.step(dve.tensor_scalar(dst, g(-1), cw[:, t, 0:1], None, ALU.mult))
                for d in (0, 1):
                    ch.step(dve.scalar_tensor_tensor(out=dst, in0=g(d), scalar=cw[:, t, d + 1:d + 2], in1=dst,
                                                     op0=ALU.mult, op1=ALU.add))
                ins = dve.tensor_tensor(dst, dst, outer[:, t, HALO:HALO + n], ALU.mult)
                ins.then_inc(out_sem, 1)
                return ins

            def windows(ch, t, n):
                m = n + META - 1
                src, d = zp[:, t, :], 1
                for g in range(4):
                    ch.step(dve.tensor_tensor(win[:, g, 0:m], src[:, 0:m], src[:, d:d + m], ALU.add))
                    src, d = win[:, g, :], 2 * d
                    m -= d

            def body(r, n, more):
                is_meta = isinstance(r, int) and r == 0
                tiles, rows, off = (1, META, 0) if is_meta else (NT, P, META)
                more = more or is_meta
                ch = Chain(dve, step, STEPS * (r - 1) if not is_meta else 0)
                if isinstance(r, int) and r:
                    ch.base = STEPS * (r - 1) + TAIL_STEPS
                for t in range(tiles):
                    for h in range(2):
                        dve.wait_ge(u_hi_made, 2 * tile(r, t) + h + 1)
                        dst = u_lo[:, 4 * h:4 * h + 4, P * t:P * t + rows]
                        dve.tensor_tensor(dst, bank[:, 6 + h, :].rearrange("p (k n) -> p k n", k=4)[:, :, 0:rows],
                                          u_hi[:, 4 * h:4 * h + 4, P * t:P * t + rows].bitcast(F32),
                                          ALU.subtract).then_inc(u_lo_made, 1)
                for t in range(3):
                    dve.wait_ge(panel_done, 12 * r + 3 * t + 2)
                    dve.wait_ge(read_act, 9 * r + 2 * t + 1)
                    dve.tensor_tensor(gated[:, t, off:off + n], bank[:, (3 * t + 1) % 4, 0:n], xa[:, 0:n],
                                      ALU.mult).then_inc(gated_made, 1)
                    dve.wait_ge(gated_made, 3 * r + t + 1)
                    if not is_meta:
                        dve.wait_ge(carried, 6 * r - 6 + t + 1)
                    dve.wait_ge(read_act, 9 * r + 2 * t + 2)
                    if is_meta:
                        dve.tensor_copy(meta3[:, 0, t, :], gated[:, t, 0:META])
                        dve.tensor_copy(meta3[:, 1, t, :], outer[:, t, 0:META]).then_inc(carried, 1)
                    else:
                        dve.wait_ge(mix_stored[t % 2], 16 * (3 * r - 3 + t // 2 + 1))
                        conv(ch, t, res[:, t % 2, :], T, mix_made)
                        dve.wait_ge(mix_made, 6 * r - 6 + t + 1)
                        dve.tensor_copy(gated[:, t, 0:META], gated[:, t, T:W])
                        dve.tensor_copy(outer[:, t, 0:META], outer[:, t, T:W]).then_inc(carried, 1)
                    if more:
                        norm(r + 1, t)
                for t in range(3):
                    dve.wait_ge(read_act, 9 * r + 6 + t + 1)
                    if is_meta:
                        dve.tensor_copy(meta3[:, 2, t, :], zp[:, t, 0:META]).then_inc(carried, 1)
                    else:
                        i = 3 + t
                        dve.wait_ge(carried, 6 * r - 6 + 3 + t + 1)
                        windows(ch, t, T)
                        dve.wait_ge(mix_stored[i % 2], 16 * (3 * r - 3 + i // 2 + 1))
                        for g, w in enumerate(WINDOWS):
                            q = slice(32 * g, 32 * g + 32)
                            ch.step(dve.scalar_tensor_tensor(
                                out=res[q, i % 2, :], in0=win[q, g, HALO - w // 2:HALO - w // 2 + T], scalar=1.0 / w,
                                in1=zp[q, t, HALO:HALO + T], op0=ALU.mult, op1=ALU.subtract))
                        dve.tensor_scalar(res[:, i % 2, :], res[:, i % 2, :], ps[:, t:t + 1], None, ALU.mult)\
                            .then_inc(mix_made, 1)
                        dve.wait_ge(mix_made, 6 * r - 6 + i + 1)
                        dve.tensor_copy(zp[:, t, 0:META], zp[:, t, T:W]).then_inc(carried, 1)
                    if more and t == 0:
                        norm(r + 1, 3)
                assert is_meta or ch.n == STEPS

            def flush(q):
                base = STEPS * (NB1 if q == 0 else NBLK) + (TAIL_STEPS if q else 0)
                ch = Chain(dve, step, base)
                dve.wait_ge(carried, 6 * (1 + (NB1 if q == 0 else NBLK)))
                for buf in (gated, outer, zp):
                    ch.step(dve.memset(buf[:, :, META:META + HALO], 0.0))
                if q:
                    dve.wait_ge(tail_stored, 16)
                for t in range(3):
                    ch.step(conv_tail(ch, t))
                for t in range(3):
                    windows(ch, t, HALO)
                    for g, w in enumerate(WINDOWS):
                        s = slice(32 * g, 32 * g + 32)
                        ch.step(dve.tensor_tensor(tail[s, 3 + t, :], win[s, g, HALO - w // 2:2 * HALO - w // 2],
                                                  icnt[s, :], ALU.mult))
                    ch.step(dve.tensor_tensor(tail[:, 3 + t, :], tail[:, 3 + t, :], zp[:, t, HALO:2 * HALO],
                                              ALU.subtract))
                    ch.step(dve.tensor_scalar(tail[:, 3 + t, :], tail[:, 3 + t, :], ps[:, t:t + 1], None, ALU.mult))
                if q == 0:
                    for b, buf in enumerate((gated, outer, zp)):
                        ch.step(dve.tensor_copy(buf[:, :, 0:META], meta3[:, b, :, :]))
                assert ch.n == TAIL_STEPS - 3 * q
                dve.engine_nop().then_inc(tail_made, 1)

            def conv_tail(ch, t):
                dst = tail[:, t, :]
                g = lambda d: gated[:, t, HALO + d:2 * HALO + d]
                ch.step(dve.tensor_scalar(dst, g(-1), cw[:, t, 0:1], None, ALU.mult))
                for d in (0, 1):
                    ch.step(dve.scalar_tensor_tensor(out=dst, in0=g(d), scalar=cw[:, t, d + 1:d + 2], in1=dst,
                                                     op0=ALU.mult, op1=ALU.add))
                return dve.tensor_tensor(dst, dst, outer[:, t, HALO:2 * HALO], ALU.mult)

            norm(0, 0, META)
            rounds(dve, body, flush)

        @block.tensor
        def _(pe):
            pe.wait_ge(consts, 16 * 8)

            def body(r, n, more):
                is_meta = isinstance(r, int) and r == 0
                tiles, rows = (1, META) if is_meta else (NT, P)
                for t in range(tiles):
                    pe.wait_ge(normed, tile(r, t) + 1)
                    for h in range(2):
                        if not is_meta:
                            pe.wait_ge(u_lo_made, 2 * tile(r, t) + h - 1)
                        for k in range(4):
                            ins = pe.transpose(bank[:, 6 + h, P * k:P * k + rows],
                                               xt[0:rows, t, (4 * h + k) * P:(4 * h + k + 1) * P],
                                               ident[0:rows, 0:rows])
                        ins.then_inc(transposed, 1)
                pe.wait_ge(u_lo_made, 2 * tile(r, tiles - 1) + 2)
                for i, j in enumerate(ORDER):
                    before = i - 4 if i >= 4 else i + 8
                    rr = r if i >= 4 else r - 1
                    if not (is_meta and i < 4):
                        if before in act_index:
                            pe.wait_ge(read_act, 9 * rr + act_index[before] + 1)
                        else:
                            pe.wait_ge(gated_made, 3 * rr + before // 3 + 1)
                    for k in range(KD):
                        ins = split_product(pe, bank[:, i % 4, 0:n], (w_hi[:, j, k, :], w_lo[:, j, k, :]),
                                            (u_hi[:, k, 0:n], u_lo[:, k, 0:n]), k == 0, k == KD - 1)
                    ins.then_inc(panel_done, 1)
                for t in range(tiles):
                    s = 1 if is_meta else t % 2
                    if not is_meta:
                        pe.wait_ge(xf_read, tile(r, t))
                    tk = slice(P * t, P * t + rows)
                    for k in range(KD):
                        wf = [w[:, NPAN + 3:NPAN + 5, k, :] for w in (w_hi, w_lo)]
                        ins = split_product(pe, bank[0:rows, 4 + s, 0:FOUR].rearrange("p (a n) -> p a n", a=2),
                                            (u_hi[:, k, tk], u_lo[:, k, tk]), wf, k == 0, k == KD - 1)
                    ins.then_inc(xf_done, 1)

            rounds(pe, body)


def fourier(nc, c, ones, half, rs):
    TILES = NT * NBLK + 1
    RING = 3
    CH = KCH
    with ExitStack() as ctx:
        sb = lambda n, s, d=F32: ctx.enter_context(nc.sbuf_tensor(n + "_sb", s, d))
        sem = lambda n: ctx.enter_context(nc.semaphore(n))
        xf = sb("xf", [P, TILES, FOUR])
        xf_hi = sb("xf_hi", [P, TILES, FOUR], F32R)
        xf_lo = sb("xf_lo", [P, TILES, FOUR], F32R)
        heads = sb("head_tables", [P, 2, P])
        b_hi = sb("head_hi", [P, 2, P], F32R)
        b_lo = sb("head_lo", [P, 2, P], F32R)
        raw = sb("table_raw", [P, RING, 2, CH])
        t_hi = sb("table_hi", [P, RING, 2, CH], F32R)
        t_lo = sb("table_lo", [P, RING, 2, CH], F32R)
        pq_hi = sb("pq_hi", [P, 4, CH], F32R)
        pq_lo = sb("pq_lo", [P, 4, CH], F32R)
        odd = sb("odd_part", [P, 2, CH])
        fwd = sb("f_forward", [P, 2, CH])
        rev = sb("f_reversed", [P, 2, CH])
        mx = sb("mix_in", [P, 4, T])
        sq = sb("mix_sq", [P, 2, T])
        ms = sb("mix_mean_sq", [P, NBLK * 12])
        bank = ctx.enter_context(nc.psum_tensor("dft_bank", [P, 8, 512], F32))

        xf_landed, consts = sem("xf_landed"), sem("head_landed")
        t_landed = [sem(f"t_landed{i}") for i in range(RING)]
        xf_hi_made, xf_lo_made = sem("xf_hi_made"), sem("xf_lo_made")
        t_hi_made, t_lo_made, t_used = sem("t_hi_made"), sem("t_lo_made"), sem("t_used")
        pq_hi_made, pq_lo_made = sem("pq_hi_made"), sem("pq_lo_made")
        head_done, odd_made, f_made = sem("head_done"), sem("odd_made"), sem("f_made")
        rev_stored, fwd_stored = sem("rev_stored"), sem("fwd_stored")
        m_landed = [sem(f"m_landed{i}") for i in range(4)]
        sq_made, sq_used, ms_made, rs_made = sem("sq_made"), sem("sq_used"), sem("ms_made"), sem("rs_made")
        block = ctx.enter_context(nc.Block())

        S1 = list(range(NT * NB1)) + [TILES - 1]
        S2 = list(range(NT * NB1, TILES))
        PER = len(S1)
        USES = [len(range(s, PER, RING)) for s in range(RING)]

        def freed(ch, i):
            if i >= RING:
                return PER * ch + i - RING + 1 + RING
            last = max(j for j in range(PER) if j % RING == i)
            return PER * ch + last - PER + 1 + RING

        def chunks(eng, step, chunk_end):
            with eng.Fori(0, NCH) as ch:
                for i, ti in enumerate(S1):
                    step(ch, i, ti, CH, 0)
                chunk_end(ch, CH, 0)
            for i, ti in enumerate(S2):
                step(NCH, i, ti, K2, 1)
            chunk_end(NCH, K2, 1)

        def rows_of(ti):
            return META if ti == TILES - 1 else P

        def token_blocks(eng, body):
            with eng.Fori(0, NBLK) as b:
                body(b, T * b + META)

        @block.sync
        def _(sp):
            for q in range(4):
                t = slice(5 * q, 5 * q + 5)
                sp.dma_start(xf[:, t, :], c["xf"][t, :, :].rearrange("t p n -> p t n")).then_inc(xf_landed, 16)
            sp.dma_start(xf[0:META, TILES - 1, :], c["xf"][TILES - 1, 0:META, :]).then_inc(xf_landed, 16)
            sp.dma_start(heads[:, :, :], c["head_tables"]).then_inc(consts, 16)

            def step(ch, i, ti, n, seq):
                sp.wait_ge(t_lo_made, freed(ch, i))
                r = rows_of(ti)
                if seq == 0:
                    src = c["table1"][bass.ds(ch, 1), i, 0:r, :].rearrange("a p n -> p (a n)")
                    dst = raw[0:r, i % RING, :, :].rearrange("p a n -> p (a n)")
                else:
                    src = c["table2"][i, 0:r, :].rearrange("p (a n) -> p a n", a=2)
                    dst = raw[0:r, i % RING, :, 0:n]
                sp.dma_start(dst, src).then_inc(t_landed[i % RING], 16)

            def chunk_end(ch, n, seq):
                sp.wait_ge(f_made, 2 * ch + 3)
                skip = 0 if seq == 0 else META - 1
                k0, r0 = (CH * ch + 1, CH * (0 - ch) + L1 - CH) if seq == 0 else (SEQ + META, SEQ + L2 - n)
                dst = c["mixT"][2 * CONV:D, :].rearrange("(m p) n -> p m n", p=P)
                sp.dma_start(dst[:, :, bass.ds(r0, n)], rev[:, :, 0:n]).then_inc(rev_stored, 16)
                sp.wait_ge(rev_stored, 16 * ch + 16)
                sp.dma_start(dst[:, :, bass.ds(k0, n - skip)], fwd[:, :, skip:n]).then_inc(fwd_stored, 16)

            sp.nop().then_inc(fwd_stored, 16)
            chunks(sp, step, chunk_end)
            sp.wait_ge(fwd_stored, 16 * (NCH + 2))

            def body(b, col):
                for k in range(KD):
                    sp.wait_ge(sq_made, 8 * b + k + 1)
                    sp.dma_start(mx[:, k % 4, :], c["mixT"][P * k:P * k + P, bass.ds(col, T)])\
                        .then_inc(m_landed[k % 4], 16)

            token_blocks(sp, body)

        @block.scalar
        def _(act):
            for q in range(4):
                act.wait_ge(xf_landed, 16 * 5)
                t = slice(5 * q, 5 * q + 5)
                act.activation(xf_hi[:, t, :], xf[:, t, :], ACT.Copy).then_inc(xf_hi_made, 1)
            act.activation(xf_hi[0:META, TILES - 1, :], xf[0:META, TILES - 1, :], ACT.Copy).then_inc(xf_hi_made, 1)
            act.wait_ge(consts, 16)
            act.activation(b_hi[:, :, :], heads[:, :, :], ACT.Copy).then_inc(xf_hi_made, 1)
            act.nop().then_inc(sq_made, 4)

            def step(ch, i, ti, n, seq):
                s, r = i % RING, rows_of(ti)
                act.wait_ge(t_landed[s], 16 * (USES[s] * ch + i // RING + 1))
                act.wait_ge(t_used, freed(ch, i))
                act.activation(t_hi[0:r, s, :, 0:n], raw[0:r, s, :, 0:n], ACT.Copy).then_inc(t_hi_made, 1)

            def chunk_end(ch, n, seq):
                act.wait_ge(t_used, (PER * ch + PER if seq == 0 else PER * NCH + len(S2)) + RING)
                for q in range(4):
                    act.activation(pq_hi[:, q, 0:n], bank[:, q, 0:n], ACT.Copy).then_inc(pq_hi_made, 1)
                act.wait_ge(f_made, 2 * ch + 1)
                for m in range(2):
                    act.wait_ge(head_done, 4 * ch + 2 * m + 2)
                    act.activation(odd[:, m, 0:n], bank[:, 6 + m, 0:n], ACT.Copy).then_inc(odd_made, 1)

            chunks(act, step, chunk_end)

            def body(b, col):
                for k in range(KD):
                    act.wait_ge(m_landed[k % 4], 16 * (2 * b + k // 4 + 1))
                    act.wait_ge(sq_used, 8 * b + k + 1)
                    act.activation(sq[:, k % 2, :], mx[:, k % 4, :], ACT.Square).then_inc(sq_made, 1)

            token_blocks(act, body)

        @block.vector
        def _(dve):
            dve.nop().then_inc(t_lo_made, RING)
            dve.nop().then_inc(pq_lo_made, 1)
            dve.nop().then_inc(f_made, 1)
            dve.nop().then_inc(ms_made, 1)
            for q in range(4):
                dve.wait_ge(xf_hi_made, q + 1)
                t = slice(5 * q, 5 * q + 5)
                dve.tensor_tensor(xf_lo[:, t, :], xf[:, t, :], xf_hi[:, t, :].bitcast(F32), ALU.subtract)\
                    .then_inc(xf_lo_made, 1)
            dve.wait_ge(xf_hi_made, 5)
            dve.tensor_tensor(xf_lo[0:META, TILES - 1, :], xf[0:META, TILES - 1, :],
                              xf_hi[0:META, TILES - 1, :].bitcast(F32), ALU.subtract).then_inc(xf_lo_made, 1)
            dve.wait_ge(xf_hi_made, 6)
            dve.tensor_tensor(b_lo[:, :, :], heads[:, :, :], b_hi[:, :, :].bitcast(F32), ALU.subtract)\
                .then_inc(xf_lo_made, 1)

            def step(ch, i, ti, n, seq):
                s, r = i % RING, rows_of(ti)
                dve.wait_ge(t_hi_made, PER * ch + i + 1)
                dve.tensor_tensor(t_lo[0:r, s, :, 0:n], raw[0:r, s, :, 0:n], t_hi[0:r, s, :, 0:n].bitcast(F32),
                                  ALU.subtract).then_inc(t_lo_made, 1)

            def chunk_end(ch, n, seq):
                for q in range(4):
                    dve.wait_ge(pq_hi_made, 4 * ch + q + 1)
                    dve.tensor_tensor(pq_lo[:, q, 0:n], bank[:, q, 0:n], pq_hi[:, q, 0:n].bitcast(F32),
                                      ALU.subtract).then_inc(pq_lo_made, 1)
                dve.wait_ge(fwd_stored, 16 * ch + 16)
                for m in range(2):
                    dve.wait_ge(odd_made, 2 * ch + m + 1)
                    dve.tensor_tensor(rev[:, m, 0:n][:, ::-1], bank[:, 4 + m, 0:n], odd[:, m, 0:n], ALU.add)
                    dve.tensor_tensor(fwd[:, m, 0:n], bank[:, 4 + m, 0:n], odd[:, m, 0:n], ALU.subtract)\
                        .then_inc(f_made, 1)

            chunks(dve, step, chunk_end)

            def body(b, col):
                dve.wait_ge(sq_used, 8 * b + 8 + 2)
                for g, width in enumerate((CONV, CONV, FOUR)):
                    ins = dve.tensor_scalar(ms[:, bass.ds(12 * b + 4 * g, 4)], bank[:, 0, 4 * g:4 * g + 4],
                                            1.0 / width, EPS, ALU.mult, ALU.add)
                ins.then_inc(ms_made, 1)

            token_blocks(dve, body)

        @block.gpsimd
        def _(pool):
            pool.wait_ge(ms_made, NBLK + 1)
            pool.tensor_tensor(rs[:, :], ms[:, :], half[:, :], ALU.pow)\
                .then_inc(rs_made, 1)

        @block.tensor
        def _(pe):
            pe.nop().then_inc(t_used, RING)
            pe.wait_ge(xf_lo_made, 6)

            def step(ch, i, ti, n, seq):
                s, r = i % RING, rows_of(ti)
                pe.wait_ge(t_lo_made, PER * ch + i + 1 + RING)
                if i == 0:
                    pe.wait_ge(pq_lo_made, 4 * ch + 1)
                last = ti == TILES - 1
                for m in range(2):
                    w = [x[0:r, ti, P * m:P * m + P] for x in (xf_hi, xf_lo)]
                    for a in range(2):
                        ins = split_product(pe, bank[:, 2 * m + a, 0:n], w,
                                            [t[0:r, s, a, 0:n] for t in (t_hi, t_lo)], i == 0, last)
                ins.then_inc(t_used, 1)

            def chunk_end(ch, n, seq):
                for m in range(2):
                    for a in range(2):
                        pe.wait_ge(pq_lo_made, 4 * ch + 2 * m + a + 2)
                        split_product(pe, bank[:, 4 + 2 * a + m, 0:n], (b_hi[:, a, :], b_lo[:, a, :]),
                                      (pq_hi[:, 2 * m + a, 0:n], pq_lo[:, 2 * m + a, 0:n]), True, True)\
                            .then_inc(head_done, 1)

            chunks(pe, step, chunk_end)
            pe.nop().then_inc(sq_used, 2)

            def body(b, col):
                pe.wait_ge(ms_made, b + 1)
                for k in range(KD):
                    g = k // 3
                    pe.wait_ge(sq_made, 8 * b + k + 1 + 4)
                    for t in range(NT):
                        ins = pe.matmul(bank[:, 0, 4 * g + t:4 * g + t + 1], sq[:, k % 2, P * t:P * t + P],
                                        ones[:, :], start=(k == 0 and t == 0), stop=(k in (2, 5, 7)),
                                        skip_group_check=True)
                    ins.then_inc(sq_used, 1)

            token_blocks(pe, body)


def finish(nc, c, ident, half, rs, eps):
    BANKS = (4, 5, 6, 7, 0, 1, 2, 3)
    RING = 4
    G0, D0 = KD, KD + 2 * MF
    PER = D0 + MF
    GROUP_OF = (0, 0, 0, 1, 1, 1, 2, 2)
    FIRST, LAST = (0, 3, 6), (2, 5, 7)
    assert G0 % RING == 0 and D0 % RING == 0
    USES = [len(range(s, PER, RING)) for s in range(RING)]
    MIX_STEP = {2 + 2 * k: k for k in range(KD)}
    with ExitStack() as ctx:
        sb = lambda n, s, d=F32: ctx.enter_context(nc.sbuf_tensor(n + "_sb", s, d))
        sem = lambda n: ctx.enter_context(nc.semaphore(n))
        w_raw = sb("w_raw", [P, RING, D])
        w_hi = sb("w_panel_hi", [P, RING, D], F32R)
        w_lo = sb("w_panel_lo", [P, RING, D], F32R)
        v_hi = sb("v_hi", [P, KD, T], F32R)
        v_lo = sb("v_lo", [P, KD, T], F32R)
        a_hi = sb("act_hi", [P, MF, T], F32R)
        a_lo = sb("act_lo", [P, MF, T], F32R)
        h = sb("h", [P, NT, D])
        stage = sb("stage", [P, 2, D])
        mx = sb("mix_raw", [P, 2, T])
        g2 = sb("norm2_rows", [P, D])
        gf = sb("final_rows", [P, D])
        mg = sb("mix_g_cols", [P, KD])
        rs_now = sb("rs_now", [P, 12])
        msq = sb("h_mean_sq", [P, NT])
        ms = sb("h_ms", [P, NT])
        rstd = sb("h_rstd", [P, NT])
        bank = ctx.enter_context(nc.psum_tensor("fin_bank", [P, 8, 512], F32))

        consts = sem("fin_consts")
        w_landed = [sem(f"w_landed{i}") for i in range(RING)]
        w_hi_made, w_lo_made, w_used = sem("w_hi_made"), sem("w_lo_made"), sem("w_used")
        h_landed = [sem(f"h_landed{i}") for i in range(NT)]
        m_landed = [sem(f"mix_landed{i}") for i in range(2)]
        m_hi_made, m_lo_made, rs_read = sem("m_hi_made"), sem("m_lo_made"), sem("rs_read")
        proj_done, proj_read = sem("proj_done"), sem("proj_read")
        squared, rstd_step, rstd_made = sem("h_squared"), sem("h_rstd_step"), sem("h_rstd_made")
        v_made, transposed = sem("v_made"), sem("v_transposed")
        v_hi_made, v_lo_made = sem("v_hi_made"), sem("v_lo_made")
        silu_made, glu_made = sem("silu_made"), sem("glu_made")
        a_hi_made, a_lo_made = sem("a_hi_made"), sem("a_lo_made")
        down_done, down_read, y_made = sem("down_done"), sem("down_read"), sem("y_made")
        y_stored = [sem(f"y_stored{i}") for i in range(2)]
        block = ctx.enter_context(nc.Block())

        def blocks(eng, body):
            with eng.Fori(0, NBLK - 1) as b:
                body(b, True)
            body(NBLK - 1, False)

        def freed(b, q):
            if not isinstance(q, int) or q >= RING:
                return PER * b + q + 1
            return PER * b + max(j for j in range(PER) if j % RING == q) - PER + 1 + RING

        def stream(b, q, more, split):
            if q + RING < PER:
                split(b, q + RING, (q + RING) % RING)
            elif more:
                split(b + 1, q + RING - PER, q + RING - PER)

        @block.sync
        def _(sp):
            for dst, name in ((g2[:, :], "norm2_rows"), (gf[:, :], "final_rows"), (mg[:, :], "mix_g_cols")):
                sp.dma_start(dst, c[name]).then_inc(consts, 16)

            def mix_load(b, k):
                sp.wait_ge(m_lo_made, KD * b + k + 1)
                sp.dma_start(mx[:, k % 2, :], c["mixT"][P * k:P * k + P, bass.ds(T * b + META, T)])\
                    .then_inc(m_landed[k % 2], 16)

            def h_load(b, t):
                sp.dma_start(h[:, t, :], c["x"][bass.ds(T * b + P * t, P), :]).then_inc(h_landed[t], 16)

            def panel(b, q, s):
                sp.wait_ge(w_lo_made, freed(b, q))
                sp.dma_start(w_raw[:, s, :], c["w_panels"][bass.ds(q, 1), :, :].rearrange("a p n -> p (a n)"))\
                    .then_inc(w_landed[s], 16)

            def body(b, more):
                for q in range(KD):
                    stream(b, q, more, panel)
                with sp.Fori(0, MF // 2) as i:
                    for s in range(RING):
                        panel(b, RING * i + G0 + RING + s, s)
                for q in range(D0, PER):
                    stream(b, q, more, panel)
                    if more and q - D0 in MIX_STEP:
                        mix_load(b + 1, MIX_STEP[q - D0])
                for t in range(NT):
                    sp.wait_ge(y_made, NT * b + t + 1)
                    sp.dma_start(c["out"][bass.ds(T * b + P * t, P), :], stage[:, t % 2, :])\
                        .then_inc(y_stored[t % 2], 16)
                    if more:
                        h_load(b + 1, t)

            for s in y_stored:
                sp.nop().then_inc(s, 16)
            for k in range(2):
                mix_load(0, k)
            for q in range(RING):
                panel(0, q, q)
            for k in range(2, KD):
                mix_load(0, k)
            for t in range(NT):
                h_load(0, t)
            blocks(sp, body)
            for s in y_stored:
                sp.wait_ge(s, 16 * (1 + 2 * NBLK))

        @block.gpsimd
        def _(pool):
            with pool.Fori(0, NBLK) as b:
                for n in range(2 * NT):
                    t = n % NT
                    pool.wait_ge(squared, 2 * NT * b + n + 1)
                    pool.tensor_tensor(ms[:, t:t + 1], msq[:, t:t + 1], eps[:, :], ALU.add).then_inc(rstd_step, 1)
                    pool.wait_ge(rstd_step, 2 * NT * b + n + 1)
                    pool.tensor_tensor(rstd[:, t:t + 1], ms[:, t:t + 1], half[:, 0:1], ALU.pow).then_inc(rstd_made, 1)

        @block.scalar
        def _(act):
            act.wait_ge(consts, 48)

            def mix_split(b, k):
                act.wait_ge(m_landed[k % 2], 16 * (KD // 2 * b + k // 2 + 1))
                act.activation(v_hi[:, k, :], mx[:, k % 2, :], ACT.Copy, scale=mg[:, k:k + 1]).then_inc(m_hi_made, 1)

            def split(b, q, s, turn=None):
                act.wait_ge(w_landed[s], 16 * (USES[s] * b + (q // RING + 1 if turn is None else turn + 1)))
                act.wait_ge(w_used, freed(b, q))
                act.activation(w_hi[:, s, :], w_raw[:, s, :], ACT.Copy).then_inc(w_hi_made, 1)

            def square(t):
                act.activation(stage[:, t % 2, :], h[:, t, :], ACT.Square, scale=D ** -0.5,
                               accum_out=msq[:, t:t + 1])\
                    .then_inc(squared, 1)

            def v_split(b, t):
                for g in range(2):
                    act.wait_ge(transposed, 2 * NT * b + 2 * t + g + 1)
                    act.activation(v_hi[:, 4 * g:4 * g + 4, P * t:P * t + P],
                                   bank[:, BANKS[2 * t + g], :].rearrange("p (k n) -> p k n", k=4),
                                   ACT.Copy).then_inc(v_hi_made, 1)

            def body(b, more):
                for q in range(KD):
                    stream(b, q, more, split)
                for t in range(NT):
                    act.wait_ge(proj_read, 24 * b + 16 + 2 * t + 2)
                    if t < 2:
                        act.wait_ge(y_stored[t], 16 * (2 * b + 1))
                    else:
                        act.wait_ge(transposed, 2 * NT * b + 2 * t - 2)
                    square(t)
                    if t:
                        v_split(b, t - 1)
                v_split(b, NT - 1)
                with act.Fori(0, MF // 2) as i:
                    for p in range(2):
                        act.wait_ge(w_used, PER * b + RING * i + 2 * p + G0 + 1 + RING)
                        act.wait_ge(a_lo_made, MF * b + 2 * i + p + 1)
                        act.activation(stage[:, p, 0:T], bank[:, 2 * p, :], ACT.Silu).then_inc(silu_made, 1)
                        for s in (2 * p, 2 * p + 1):
                            split(b, RING * i + G0 + RING + s, s, i + G0 // RING + 1)
                        act.wait_ge(glu_made, MF * b + 2 * i + p + 3)
                        act.activation(a_hi[:, bass.ds(2 * i + p, 1), :].rearrange("p a n -> p (a n)"),
                                       stage[:, p, 0:T], ACT.Copy).then_inc(a_hi_made, 1)
                for q in range(D0, PER):
                    stream(b, q, more, split)
                    if more and q - D0 in MIX_STEP:
                        mix_split(b + 1, MIX_STEP[q - D0])
                for t in range(NT):
                    act.wait_ge(down_read, 8 * b + 8 + 2 * t + 2)
                    if t >= 2:
                        act.wait_ge(y_stored[t % 2], 16 * (2 * b + 2))
                    square(t)

            for q in range(RING):
                split(0, q, q)
            for k in range(KD):
                mix_split(0, k)
            blocks(act, body)

        @block.vector
        def _(dve):
            dve.nop().then_inc(w_lo_made, RING)
            dve.nop().then_inc(m_lo_made, 2)
            dve.nop().then_inc(glu_made, 2)
            dve.nop().then_inc(a_lo_made, 2)
            dve.nop().then_inc(down_read, 8)
            dve.wait_ge(consts, 48)

            def mix_split(b, k):
                dve.wait_ge(m_hi_made, KD * b + k + 1)
                dve.scalar_tensor_tensor(out=v_lo[:, k, :], in0=mx[:, k % 2, :], scalar=mg[:, k:k + 1],
                                         in1=v_hi[:, k, :].bitcast(F32), op0=ALU.mult, op1=ALU.subtract)\
                    .then_inc(m_lo_made, 1)

            def split(b, q, s):
                dve.wait_ge(w_hi_made, PER * b + q + 1)
                dve.tensor_tensor(w_lo[:, s, :], w_raw[:, s, :], w_hi[:, s, :].bitcast(F32), ALU.subtract)\
                    .then_inc(w_lo_made, 1)

            def proj_add(b, g, j):
                t, n = j // 2, j % 2
                if j < 7:
                    dve.wait_ge(proj_done, 21 * b + 7 * g + j + 1)
                else:
                    dve.wait_ge(w_used, PER * b + LAST[g] + 1 + RING)
                part = h[:, t, 512 * n:512 * n + 512]
                if g == 0:
                    dve.wait_ge(h_landed[t], 16 * b + 16)
                else:
                    dve.wait_ge(proj_read, 24 * b + 8 * g - 8 + j + 1)
                dve.scalar_tensor_tensor(out=part, in0=bank[:, BANKS[j], :], scalar=rs_now[:, 4 * g + t:4 * g + t + 1],
                                         in1=part, op0=ALU.mult, op1=ALU.add).then_inc(proj_read, 1)

            def v_norm(b, t):
                dve.wait_ge(rstd_made, 2 * NT * b + t + 1)
                dve.scalar_tensor_tensor(out=stage[:, t % 2, :], in0=h[:, t, :], scalar=rstd[:, t:t + 1],
                                         in1=g2[:, :], op0=ALU.mult, op1=ALU.mult).then_inc(v_made, 1)

            def v_split(b, t):
                for g in range(2):
                    dve.wait_ge(v_hi_made, 2 * NT * b + 2 * t + g + 1)
                    to = (slice(None), slice(4 * g, 4 * g + 4), slice(P * t, P * t + P))
                    dve.tensor_tensor(v_lo[to], bank[:, BANKS[2 * t + g], :].rearrange("p (k n) -> p k n", k=4),
                                      v_hi[to].bitcast(F32), ALU.subtract).then_inc(v_lo_made, 1)

            def y_norm(b, t):
                dve.wait_ge(rstd_made, 2 * NT * b + NT + t + 1)
                dve.scalar_tensor_tensor(out=stage[:, t % 2, :], in0=h[:, t, :], scalar=rstd[:, t:t + 1],
                                         in1=gf[:, :], op0=ALU.mult, op1=ALU.mult).then_inc(y_made, 1)

            def body(b, more):
                dve.tensor_copy(rs_now[:, :], rs[:, bass.ds(12 * b, 12)]).then_inc(rs_read, 1)
                dve.wait_ge(rs_read, b + 1)
                for q in range(KD):
                    stream(b, q, more, split)
                    if q in LAST[:2]:
                        for j in range(8):
                            proj_add(b, GROUP_OF[q], j)
                proj_tile = lambda t: [proj_add(b, 2, j) for j in (2 * t, 2 * t + 1)]
                proj_tile(0)
                proj_tile(1)
                v_norm(b, 0)
                proj_tile(2)
                v_norm(b, 1)
                v_split(b, 0)
                proj_tile(3)
                v_norm(b, 2)
                v_split(b, 1)
                v_norm(b, 3)
                v_split(b, 2)
                v_split(b, 3)
                with dve.Fori(0, MF // 2) as i:
                    for p in range(2):
                        m = 2 * i + p
                        split(b, RING * i + G0 + RING + 2 * p, 2 * p)
                        dve.wait_ge(silu_made, MF * b + m + 1)
                        dve.wait_ge(w_used, PER * b + RING * i + 2 * p + G0 + 2 + RING)
                        dve.tensor_tensor(stage[:, p, 0:T], bank[:, 2 * p + 1, :], stage[:, p, 0:T], ALU.mult)\
                            .then_inc(glu_made, 1)
                        split(b, RING * i + G0 + RING + 2 * p + 1, 2 * p + 1)
                        dve.wait_ge(a_hi_made, MF * b + m + 1)
                        at = lambda a: a[:, bass.ds(m, 1), :].rearrange("p a n -> p (a n)")
                        dve.tensor_tensor(at(a_lo), stage[:, p, 0:T], at(a_hi).bitcast(F32), ALU.subtract)\
                            .then_inc(a_lo_made, 1)
                for q in range(D0, PER):
                    stream(b, q, more, split)
                    if more and q - D0 in MIX_STEP:
                        mix_split(b + 1, MIX_STEP[q - D0])
                for t in range(NT):
                    for j in (2 * t, 2 * t + 1):
                        if j < 7:
                            dve.wait_ge(down_done, 7 * b + j + 1)
                        else:
                            dve.wait_ge(w_used, PER * b + PER + RING)
                        part = h[:, t, 512 * (j % 2):512 * (j % 2) + 512]
                        dve.tensor_tensor(part, bank[:, BANKS[j], :], part, ALU.add).then_inc(down_read, 1)
                    if t:
                        y_norm(b, t - 1)
                y_norm(b, NT - 1)

            for q in range(RING):
                split(0, q, q)
            for k in range(KD):
                mix_split(0, k)
            blocks(dve, body)

        @block.tensor
        def _(pe):
            pe.nop().then_inc(w_used, RING)

            def rows(b, q, s, src, k, first, last, done):
                pe.wait_ge(w_lo_made, PER * b + q + 1 + RING)
                for j in range(8):
                    if first:
                        if done is proj_done:
                            g = GROUP_OF[k]
                            if g == 0:
                                pe.wait_ge(down_read, 8 * b + j + 1)
                            else:
                                pe.wait_ge(proj_read, 24 * b + 8 * g - 8 + j + 1)
                        elif BANKS[j] < 4:
                            pe.wait_ge(glu_made, MF * b + MF + 2)
                    t, n = j // 2, j % 2
                    ins = split_product(pe, bank[:, BANKS[j], :], [x[:, k, P * t:P * t + P] for x in src],
                                        [w[:, s, 512 * n:512 * n + 512] for w in (w_hi, w_lo)], first, last)
                    if last and j < 7:
                        ins.then_inc(done, 1)
                ins.then_inc(w_used, 1)

            def body(b, more):
                for k in range(KD):
                    if k == 0:
                        pe.wait_ge(m_lo_made, KD * b + KD + 2)
                    rows(b, k, k % RING, (v_hi, v_lo), k, k in FIRST, k in LAST, proj_done)
                for t in range(NT):
                    pe.wait_ge(v_made, NT * b + t + 1)
                    for g in range(2):
                        for k in range(4):
                            ins = pe.transpose(bank[:, BANKS[2 * t + g], P * k:P * k + P],
                                               stage[:, t % 2, (4 * g + k) * P:(4 * g + k + 1) * P], ident[:, :])
                        ins.then_inc(transposed, 1)
                with pe.Fori(0, MF // 2) as i:
                    pe.wait_ge(v_lo_made, 2 * NT * (b + 1))
                    for p in range(2):
                        pe.wait_ge(glu_made, MF * b + 2 * i + p + 1)
                        for s in (2 * p, 2 * p + 1):
                            pe.wait_ge(w_lo_made, PER * b + RING * i + G0 + s + 1 + RING)
                            for k in range(KD):
                                ins = split_product(pe, bank[:, s, :],
                                                    [w[:, s, P * k:P * k + P] for w in (w_hi, w_lo)],
                                                    (v_hi[:, k, :], v_lo[:, k, :]), k == 0, k == KD - 1)
                            ins.then_inc(w_used, 1)
                for k in range(MF):
                    if k == 0:
                        pe.wait_ge(a_lo_made, MF * (b + 1) + 2)
                    rows(b, D0 + k, (D0 + k) % RING, (a_hi, a_lo), k, k == 0, k == MF - 1, down_done)

            blocks(pe, body)


def build(nc, c):
    with ExitStack() as ctx:
        ident = ctx.enter_context(nc.sbuf_tensor("ident_sb", [P, P], F32))
        half = ctx.enter_context(nc.sbuf_tensor("minus_half_sb", [P, 12 * NBLK], F32))
        ones = ctx.enter_context(nc.sbuf_tensor("ones_sb", [P, 1], F32))
        eps = ctx.enter_context(nc.sbuf_tensor("eps_sb", [P, 1], F32))
        rs = ctx.enter_context(nc.sbuf_tensor("group_rstd", [P, 12 * NBLK], F32))
        with nc.sbuf_tensor("w_in_hi", [P, NPAN + 5, KD, P], F32R) as w_hi, \
                nc.sbuf_tensor("w_in_lo", [P, NPAN + 5, KD, P], F32R) as w_lo:
            prepare(nc, c, w_hi, w_lo)
            project(nc, c, w_hi, w_lo, ident, half, ones, eps)
        fourier(nc, c, ones, half, rs)
        finish(nc, c, ident, half, rs, eps)


def dft_tables(length, rows, freqs):
    turns = (rows[:, None] * freqs[None, :]) % length * (2 * np.pi / length)
    return (np.stack([np.cos(turns), np.sin(turns)], axis=1) / np.sqrt(length)).astype(np.float32)


def constants():
    k = {"ident": np.eye(P, dtype=np.float32), "minus_half": np.full((P, 12 * NBLK), -0.5, np.float32),
         "ones": np.ones((P, 1), np.float32), "eps": np.full((P, 1), EPS, np.float32)}
    back = np.arange(8)[::-1]
    k["inv_counts"] = np.repeat(np.stack([1.0 / (np.minimum(w - 1 - w // 2, back) + w // 2 + 1) for w in WINDOWS]),
                                32, axis=0).astype(np.float32)
    dims = np.arange(HD)
    head = dft_tables(HD, dims, dims)
    tables = np.zeros((P, 2, P), np.float32)
    for n in range(P // HD):
        tables[HD * n:HD * n + HD, :, HD * n:HD * n + HD] = head
    k["head_tables"] = tables
    for name, length, freqs, chunks in (("table1", L1, NCH * KCH, NCH), ("table2", L2, K2, 1)):
        at = np.arange(META, length)
        width = freqs // chunks
        out = np.zeros((chunks, (length - META) // P + 1, P, 2 * width), np.float32)
        for n in range(chunks):
            f = np.arange(1 + n * width, 1 + (n + 1) * width)
            out[n, :-1] = dft_tables(length, at, f).reshape(-1, P, 2 * width)
            out[n, -1, 0:META] = dft_tables(length, np.arange(META), f).reshape(META, 2 * width)
        k[name] = out if chunks > 1 else out[0]
    return k


def kernel(x_prompt, x_sample, meta_tokens, norm1_g, w_in, conv_w, pool_w, pool_scale, mix_g, w_out, norm2_g,
           w_gate_up, w_down, final_g):
    import concourse.bacc as bacc
    from concourse.bass_utils import run_bass_kernel_spmd

    asc = np.ascontiguousarray
    x_prompt, x_sample, w_in, w_out, w_gu, w_down = (
        np.asarray(a) for a in (x_prompt, x_sample, w_in[0], w_out[0], w_gate_up[0], w_down[0]))
    arrays = constants()
    arrays["x"] = np.concatenate([x_prompt[0], x_sample[0]])
    arrays["meta"] = np.asarray(meta_tokens)
    for name, g in (("norm1_rows", norm1_g[0]), ("norm2_rows", norm2_g[0]), ("final_rows", final_g)):
        arrays[name] = asc(np.broadcast_to(np.asarray(g), (P, D)))

    def column_panels(w):
        return asc(w.reshape(KD, P, -1, P).transpose(2, 1, 0, 3)).reshape(-1, P, D)

    four = column_panels(w_in[:, 3 * CONV + CONV:])
    arrays["w_in_panels"] = np.concatenate([column_panels(w_in[:, 0:3 * CONV]), four])
    arrays["w_pool_T"] = asc(w_in[:, 3 * CONV:4 * CONV].T).reshape(4, GROUP, D)
    arrays["pool_w"] = asc(np.asarray(pool_w[0]))
    arrays["conv_cols"] = asc(np.asarray(conv_w[0]).reshape(3, 3, P).transpose(2, 1, 0))

    def pool_order(a):
        return a.reshape(4, 3, 32, -1).transpose(1, 0, 2, 3).reshape(CONV, -1)

    def mixed(a):
        a = np.asarray(a).reshape(D, -1)
        return np.concatenate([a[0:CONV], pool_order(a[CONV:2 * CONV]), a[2 * CONV:]])

    arrays["pool_scale_cols"] = asc(pool_order(np.asarray(pool_scale[0])).reshape(3, P).T)
    arrays["mix_g_cols"] = asc(mixed(mix_g[0]).reshape(KD, P).T)
    gate, up = column_panels(w_gu[:, 0:DFF]), column_panels(w_gu[:, DFF:])
    arrays["w_panels"] = np.concatenate([mixed(w_out).reshape(KD, P, D),
                                         np.stack([gate, up], axis=1).reshape(-1, P, D),
                                         w_down.reshape(MF, P, D)])

    nc = bacc.Bacc("TRN2", target_bir_lowering=False, num_devices=1)
    c = {n: nc.dram_tensor(n, list(a.shape), F32, kind="ExternalInput").ap() for n, a in arrays.items()}
    c["mixT"] = nc.dram_tensor("mixT", [D, META + SEQ + DEC], F32).ap()
    c["xf"] = nc.dram_tensor("xf", [NT * NBLK + 1, P, FOUR], F32).ap()
    c["out"] = nc.dram_tensor("out", [SEQ + DEC, D], F32, kind="ExternalOutput").ap()
    build(nc, c)
    r = run_bass_kernel_spmd(nc, [arrays], core_ids=[0])
    out = r.results[0]["out"]
    return out[None, 0:SEQ], out[None, SEQ:]
```

```python
from contextlib import ExitStack

import numpy as np

import concourse.bass as bass
from concourse import mybir
from concourse.alu_op_type import AluOpType as ALU

ACT = mybir.ActivationFunctionType
F32 = mybir.dt.float32
F32R = mybir.dt.float32r

P = 128
D = 1024
KD = D // P
META = 16
SEQ, DEC = 2048, 512
L1, L2 = META + SEQ, META + DEC
T = 512
NT = T // P
NB1 = SEQ // T
NBLK = (SEQ + DEC) // T
CONV = 3 * D // 8
GROUP = CONV // 4
FOUR = D - 2 * CONV
HD = FOUR // 4
DFF = -(-8 * D // (3 * 256)) * 256
MF = DFF // P
EPS = 1e-6
NPAN = 3 * CONV // P
KCH = 344
NCH = 3
K2 = L2 // 2
WINDOWS = (2, 4, 8, 16)
UNITS = 4 + MF + MF // 2
assert NCH * KCH == L1 // 2 and DFF % 256 == 0 and UNITS % 2 == 1


def split_product(pe, out, w, x, first, last):
    pe.matmul(out, w[0], x[0], start=first, stop=False, skip_group_check=True)
    pe.matmul(out, w[0], x[1], start=False, stop=False, skip_group_check=True)
    return pe.matmul(out, w[1], x[0], start=False, stop=last, skip_group_check=True)


class Chain:

    def __init__(self, eng, sem, base=0):
        self.eng, self.sem, self.base, self.n = eng, sem, base, 0

    def step(self, ins):
        self.n += 1
        ins.then_inc(self.sem, 1)
        self.eng.wait_ge(self.sem, self.base + self.n)


def prepare(nc, c, w_hi, w_lo):
    RAW = 3
    with ExitStack() as ctx:
        sb = lambda n, s, d=F32: ctx.enter_context(nc.sbuf_tensor(n + "_sb", s, d))
        sem = lambda n: ctx.enter_context(nc.semaphore(n))
        raw = sb("raw_panel", [P, RAW, D])
        wp = sb("w_pool_T", [GROUP, 4, D])
        pw = sb("pool_w", [GROUP, 4, GROUP])
        bank = ctx.enter_context(nc.psum_tensor("fold_bank", [P, 8, 512], F32))
        raw_landed = [sem(f"raw_landed{i}") for i in range(RAW)]
        wp_landed = sem("wp_landed")
        hi_made, lo_made = sem("hi_made"), sem("lo_made")
        fold_done, fold_hi = sem("fold_done"), sem("fold_hi")
        panels = [j for j in range(NPAN)] + [NPAN + 3, NPAN + 4]
        block = ctx.enter_context(nc.Block())

        def folded(w, g, h):
            return w[:, NPAN:NPAN + 3, 4 * h:4 * h + 4, 32 * g:32 * g + 32]

        def fold_bank(g, h):
            return bank[:, 2 * g + h, 0:4 * GROUP].rearrange("p (k t j) -> p t k j", k=4, t=3)

        @block.sync
        def _(sp):
            sp.dma_start(wp[:, :, :], c["w_pool_T"].rearrange("g j k -> j g k")).then_inc(wp_landed, 16)
            sp.dma_start(pw[:, :, :], c["pool_w"].rearrange("g j o -> j g o")).then_inc(wp_landed, 16)
            for n, j in enumerate(panels):
                if n >= RAW:
                    sp.wait_ge(lo_made, n - RAW + 1)
                src = c["w_in_panels"][n, :, :]
                sp.dma_start(raw[:, n % RAW, :], src).then_inc(raw_landed[n % RAW], 16)

        @block.scalar
        def _(act):
            for n, j in enumerate(panels):
                act.wait_ge(raw_landed[n % RAW], 16 * (n // RAW + 1))
                act.activation(w_hi[:, j, :, :], raw[:, n % RAW, :].rearrange("p (k n) -> p k n", k=KD),
                               ACT.Copy).then_inc(hi_made, 1)
                if n == 5:
                    for g in range(4):
                        for h in range(2):
                            act.wait_ge(fold_done, 2 * g + h + 1)
                            for t in range(3):
                                ins = act.activation(folded(w_hi, g, h)[:, t], fold_bank(g, h)[:, t], ACT.Copy)
                            ins.then_inc(fold_hi, 1)

        @block.vector
        def _(dve):
            for n, j in enumerate(panels):
                dve.wait_ge(hi_made, n + 1)
                dve.tensor_tensor(w_lo[:, j, :, :], raw[:, n % RAW, :].rearrange("p (k n) -> p k n", k=KD),
                                  w_hi[:, j, :, :].bitcast(F32), ALU.subtract).then_inc(lo_made, 1)
                if n == 5:
                    for g in range(4):
                        for h in range(2):
                            dve.wait_ge(fold_hi, 2 * g + h + 1)
                            for t in range(3):
                                dve.tensor_tensor(folded(w_lo, g, h)[:, t], fold_bank(g, h)[:, t],
                                                  folded(w_hi, g, h)[:, t].bitcast(F32), ALU.subtract)

        @block.tensor
        def _(pe):
            pe.wait_ge(wp_landed, 32)
            for g in range(4):
                for h in range(2):
                    for k in range(4):
                        ins = pe.matmul(bank[:, 2 * g + h, k * GROUP:(k + 1) * GROUP],
                                        wp[:, g, (4 * h + k) * P:(4 * h + k + 1) * P], pw[:, g, :],
                                        start=True, stop=True)
                    ins.then_inc(fold_done, 1)


def project(nc, c, w_hi, w_lo, ident, half, eps):
    HALO = 8
    W = META + T
    ROUNDS = NBLK + 1
    with ExitStack() as ctx:
        sb = lambda n, s, d=F32: ctx.enter_context(nc.sbuf_tensor(n + "_sb", s, d))
        sem = lambda n: ctx.enter_context(nc.semaphore(n))
        u_hi = sb("u_hi", [P, KD, T], F32R)
        u_lo = sb("u_lo", [P, KD, T], F32R)
        xt = sb("x_tiles", [P, NT, D])
        junk = sb("junk", [P, D])
        g1 = sb("norm1_rows", [P, D])
        msq = sb("mean_sq", [P, NT])
        ms = sb("mean_sq_eps", [P, NT])
        rstd = sb("rstd", [P, NT])
        xa = sb("xa", [P, T])
        gated = sb("gated", [P, 3, W])
        outer = sb("outer_gate", [P, 3, W])
        zp = sb("z_pool", [P, 3, W])
        meta3 = sb("meta3", [P, 3, 3, META])
        win = sb("window_sums", [P, 4, W])
        res = sb("mix_tiles", [P, 2, T])
        tail = sb("mix_tails", [P, 6, HALO])
        cw = sb("conv_w", [P, 3, 3])
        ps = sb("pool_scale", [P, 3])
        icnt = sb("inv_counts", [P, HALO])
        xf_st = sb("xf_stage", [P, 2, FOUR])
        bank = ctx.enter_context(nc.psum_tensor("proj_bank", [P, 8, 512], F32))

        consts = sem("consts_landed")
        landed = [sem(f"x_landed{i}") for i in range(NT)]
        squared, rstd_made, rstd_step, normed = sem("squared"), sem("rstd_made"), sem("rstd_step"), sem("normed")
        transposed, u_hi_made, u_lo_made = sem("transposed"), sem("u_hi_made"), sem("u_lo_made")
        panel_done, read_act, gated_made = sem("panel_done"), sem("read_act"), sem("gated_made")
        carried, step = sem("carried"), sem("vector_step")
        mix_made = sem("mix_made")
        mix_stored = [sem(f"mix_stored{i}") for i in range(2)]
        tail_made, tail_stored = sem("tail_made"), sem("tail_stored")
        xf_done, xf_read = sem("xf_done"), sem("xf_read")
        xf_stored = [sem(f"xf_stored{i}") for i in range(2)]
        block = ctx.enter_context(nc.Block())

        ORDER = [q for t in range(3) for q in (t, 6 + t, 3 + t)] + [NPAN + t for t in range(3)]
        READS = {0: "act", 1: "dve", 2: "act"}
        act_index = {}
        for i in range(12):
            if i >= 9 or i % 3 != 1:
                act_index[i] = len(act_index)

        def tile(r, t):
            return 4 * r - 3 + t if not isinstance(r, int) or r else 0

        def rounds(eng, body, flush=None):
            body(0, META, False)
            with eng.Fori(1, NB1 + 1) as r:
                body(r, T, True)
            if flush:
                flush(0)
            body(NB1 + 1, T, False)
            if flush:
                flush(1)

        @block.sync
        def _(sp):
            for dst, name in ((ident[:, :], "ident"), (g1[:, :], "norm1_rows"), (cw[:, :, :], "conv_cols"),
                              (ps[:, :], "pool_scale_cols"), (icnt[:, :], "inv_counts"),
                              (half[:, :], "minus_half"), (eps[:, :], "eps")):
                sp.dma_start(dst, c[name]).then_inc(consts, 16)
            sp.dma_start(xt[0:META, 0, :], c["meta"]).then_inc(landed[0], 16)
            for s in (*mix_stored, *xf_stored):
                sp.nop().then_inc(s, 16)

            def load(r, t):
                if not (isinstance(r, int) and r == 0 and t):
                    sp.wait_ge(transposed, 2 * tile(r, t) + 2)
                row = T * r + P * t
                sp.dma_start(xt[:, t, :], c["x"][bass.ds(row, P), :]).then_inc(landed[t], 16)

            def body(r, n, more):
                if more or isinstance(r, int) and r == 0:
                    for t in range(NT):
                        load(r, t)
                is_meta = isinstance(r, int) and r == 0
                last = isinstance(r, int) and r
                if not is_meta:
                    col, skip = (META + SEQ, HALO) if last else (T * r - T + HALO, 0)
                    for i in range(6):
                        sp.wait_ge(mix_made, 6 * r - 6 + i + 1)
                        sp.dma_start(c["mixT"][P * i:P * i + P, bass.ds(col, T - skip)], res[:, i % 2, skip:T])\
                            .then_inc(mix_stored[i % 2], 16)
                for t in range(1 if is_meta else NT):
                    s = 1 if is_meta else t % 2
                    sp.wait_ge(xf_read, tile(r, t) + 2)
                    if is_meta:
                        sp.dma_start(c["xf"][NT * NBLK, 0:META, :], xf_st[0:META, s, :]).then_inc(xf_stored[s], 16)
                    else:
                        sp.dma_start(c["xf"][bass.ds(4 * r - 4 + t, 1), :, :].rearrange("a p n -> p (a n)"),
                                     xf_st[:, s, :]).then_inc(xf_stored[s], 16)

            def flush(q):
                sp.wait_ge(tail_made, q + 1)
                col = META + (SEQ, SEQ + DEC)[q] - HALO
                sp.dma_start(c["mixT"][0:6 * P, col:col + HALO].rearrange("(i p) n -> p i n", p=P),
                             tail[:, :, :]).then_inc(tail_stored, 16)

            rounds(sp, body, flush)
            sp.wait_ge(tail_stored, 32)
            for s in mix_stored:
                sp.wait_ge(s, 16 * (1 + 3 * NBLK))
            sp.wait_ge(xf_stored[0], 16 * (1 + 2 * NBLK))
            sp.wait_ge(xf_stored[1], 16 * (2 + 2 * NBLK))

        @block.gpsimd
        def _(pool):
            pool.wait_ge(consts, 16 * 7)

            def rms(n, rows, t):
                pool.wait_ge(squared, n + 1)
                pool.tensor_tensor(ms[0:rows, t:t + 1], msq[0:rows, t:t + 1], eps[0:rows, :], ALU.add)\
                    .then_inc(rstd_step, 1)
                pool.wait_ge(rstd_step, n + 1)
                pool.tensor_tensor(rstd[0:rows, t:t + 1], ms[0:rows, t:t + 1], half[0:rows, 0:1], ALU.pow)\
                    .then_inc(rstd_made, 1)

            rms(0, META, 0)
            with pool.Fori(1, NBLK + 1) as r:
                for t in range(NT):
                    rms(tile(r, t), P, t)

        @block.scalar
        def _(act):
            act.wait_ge(consts, 16 * 7)
            act.nop().then_inc(xf_read, 1)

            def square(r, t, rows=P):
                n = tile(r, t)
                act.wait_ge(landed[t], 16 * (r + (t == 0)) if not isinstance(r, int) or r else 16)
                if not isinstance(r, int) or r:
                    act.wait_ge(squared, n)
                act.activation(junk[0:rows, :], xt[0:rows, t, :], ACT.Square, scale=D ** -0.5,
                               accum_out=msq[0:rows, t:t + 1]).then_inc(squared, 1)

            def body(r, n, more):
                is_meta = isinstance(r, int) and r == 0
                last = isinstance(r, int) and r
                tiles, rows, off = (1, META, 0) if is_meta else (NT, P, META)
                more = more or is_meta
                for t in range(tiles):
                    for h in range(2):
                        act.wait_ge(transposed, 2 * tile(r, t) + h + 1)
                        act.activation(u_hi[:, 4 * h:4 * h + 4, P * t:P * t + rows],
                                       bank[:, 6 + h, :].rearrange("p (k n) -> p k n", k=4)[:, :, 0:rows],
                                       ACT.Copy).then_inc(u_hi_made, 1)
                for i in range(12):
                    q, t = i % 3, i // 3 if i < 9 else i - 9
                    if i < 9 and q == 1:
                        continue
                    act.wait_ge(panel_done, 12 * r + i + 1)
                    if i < 9 and q == 0:
                        dst = xa[:, 0:n]
                        if not (is_meta and t == 0):
                            act.wait_ge(gated_made, 3 * r + t)
                    elif i < 9:
                        dst = outer[:, t, off:off + n]
                        if not is_meta:
                            act.wait_ge(carried, 6 * r - 6 + t + 1)
                    else:
                        dst = zp[:, t, off:off + n]
                        if not is_meta:
                            act.wait_ge(carried, 6 * r - 6 + 3 + t + 1)
                    if last and i == 2:
                        act.wait_ge(tail_made, 1)
                    act.activation(dst, bank[:, i % 4, 0:n], ACT.Copy).then_inc(read_act, 1)
                    if more and i in (2, 5, 8, 9):
                        t2 = {2: 0, 5: 1, 8: 2, 9: 3}[i]
                        square(r + 1, t2)
                for t in range(tiles):
                    s = 1 if is_meta else t % 2
                    act.wait_ge(xf_done, tile(r, t) + 1)
                    if is_meta:
                        act.wait_ge(xf_stored[s], 16)
                    elif s == 0:
                        act.wait_ge(xf_stored[s], 16 * (2 * r - 2 + t // 2 + 1))
                    else:
                        act.wait_ge(xf_stored[s], 16 * (2 * r - 2 + t // 2 + 2))
                    act.activation(xf_st[0:rows, s, :], bank[0:rows, 4 + s, 0:FOUR], ACT.Copy).then_inc(xf_read, 1)

            square(0, 0, META)
            rounds(act, body)

        @block.vector
        def _(dve):
            dve.wait_ge(consts, 16 * 7)
            STEPS = 3 * 3 + 3 * 8
            TAIL_STEPS = 3 + 3 * 4 + 3 * 10 + 3

            def norm(r, t, rows=P):
                dve.wait_ge(rstd_made, tile(r, t) + 1)
                dve.scalar_tensor_tensor(out=xt[0:rows, t, :], in0=xt[0:rows, t, :], scalar=rstd[0:rows, t:t + 1],
                                         in1=g1[0:rows, :], op0=ALU.mult, op1=ALU.mult).then_inc(normed, 1)

            def conv(ch, t, dst, n, out_sem):
                g = lambda d: gated[:, t, HALO + d:HALO + d + n]
                ch.step(dve.tensor_scalar(dst, g(-1), cw[:, t, 0:1], None, ALU.mult))
                for d in (0, 1):
                    ch.step(dve.scalar_tensor_tensor(out=dst, in0=g(d), scalar=cw[:, t, d + 1:d + 2], in1=dst,
                                                     op0=ALU.mult, op1=ALU.add))
                ins = dve.tensor_tensor(dst, dst, outer[:, t, HALO:HALO + n], ALU.mult)
                ins.then_inc(out_sem, 1)
                return ins

            def windows(ch, t, n):
                m = n + META - 1
                src, d = zp[:, t, :], 1
                for g in range(4):
                    ch.step(dve.tensor_tensor(win[:, g, 0:m], src[:, 0:m], src[:, d:d + m], ALU.add))
                    src, d = win[:, g, :], 2 * d
                    m -= d

            def body(r, n, more):
                is_meta = isinstance(r, int) and r == 0
                tiles, rows, off = (1, META, 0) if is_meta else (NT, P, META)
                more = more or is_meta
                ch = Chain(dve, step, STEPS * (r - 1) if not is_meta else 0)
                if isinstance(r, int) and r:
                    ch.base = STEPS * (r - 1) + TAIL_STEPS
                for t in range(tiles):
                    for h in range(2):
                        dve.wait_ge(u_hi_made, 2 * tile(r, t) + h + 1)
                        dst = u_lo[:, 4 * h:4 * h + 4, P * t:P * t + rows]
                        dve.tensor_tensor(dst, bank[:, 6 + h, :].rearrange("p (k n) -> p k n", k=4)[:, :, 0:rows],
                                          u_hi[:, 4 * h:4 * h + 4, P * t:P * t + rows].bitcast(F32),
                                          ALU.subtract).then_inc(u_lo_made, 1)
                for t in range(3):
                    dve.wait_ge(panel_done, 12 * r + 3 * t + 2)
                    dve.wait_ge(read_act, 9 * r + 2 * t + 1)
                    dve.tensor_tensor(gated[:, t, off:off + n], bank[:, (3 * t + 1) % 4, 0:n], xa[:, 0:n],
                                      ALU.mult).then_inc(gated_made, 1)
                    dve.wait_ge(gated_made, 3 * r + t + 1)
                    if not is_meta:
                        dve.wait_ge(carried, 6 * r - 6 + t + 1)
                    dve.wait_ge(read_act, 9 * r + 2 * t + 2)
                    if is_meta:
                        dve.tensor_copy(meta3[:, 0, t, :], gated[:, t, 0:META])
                        dve.tensor_copy(meta3[:, 1, t, :], outer[:, t, 0:META]).then_inc(carried, 1)
                    else:
                        dve.wait_ge(mix_stored[t % 2], 16 * (3 * r - 3 + t // 2 + 1))
                        conv(ch, t, res[:, t % 2, :], T, mix_made)
                        dve.wait_ge(mix_made, 6 * r - 6 + t + 1)
                        dve.tensor_copy(gated[:, t, 0:META], gated[:, t, T:W])
                        dve.tensor_copy(outer[:, t, 0:META], outer[:, t, T:W]).then_inc(carried, 1)
                    if more:
                        norm(r + 1, t)
                for t in range(3):
                    dve.wait_ge(read_act, 9 * r + 6 + t + 1)
                    if is_meta:
                        dve.tensor_copy(meta3[:, 2, t, :], zp[:, t, 0:META]).then_inc(carried, 1)
                    else:
                        i = 3 + t
                        dve.wait_ge(carried, 6 * r - 6 + 3 + t + 1)
                        windows(ch, t, T)
                        dve.wait_ge(mix_stored[i % 2], 16 * (3 * r - 3 + i // 2 + 1))
                        for g, w in enumerate(WINDOWS):
                            q = slice(32 * g, 32 * g + 32)
                            ch.step(dve.scalar_tensor_tensor(
                                out=res[q, i % 2, :], in0=win[q, g, HALO - w // 2:HALO - w // 2 + T], scalar=1.0 / w,
                                in1=zp[q, t, HALO:HALO + T], op0=ALU.mult, op1=ALU.subtract))
                        dve.tensor_scalar(res[:, i % 2, :], res[:, i % 2, :], ps[:, t:t + 1], None, ALU.mult)\
                            .then_inc(mix_made, 1)
                        dve.wait_ge(mix_made, 6 * r - 6 + i + 1)
                        dve.tensor_copy(zp[:, t, 0:META], zp[:, t, T:W]).then_inc(carried, 1)
                    if more and t == 0:
                        norm(r + 1, 3)
                assert is_meta or ch.n == STEPS

            def flush(q):
                base = STEPS * (NB1 if q == 0 else NBLK) + (TAIL_STEPS if q else 0)
                ch = Chain(dve, step, base)
                dve.wait_ge(carried, 6 * (1 + (NB1 if q == 0 else NBLK)))
                for buf in (gated, outer, zp):
                    ch.step(dve.memset(buf[:, :, META:META + HALO], 0.0))
                if q:
                    dve.wait_ge(tail_stored, 16)
                for t in range(3):
                    ch.step(conv_tail(ch, t))
                for t in range(3):
                    windows(ch, t, HALO)
                    for g, w in enumerate(WINDOWS):
                        s = slice(32 * g, 32 * g + 32)
                        ch.step(dve.tensor_tensor(tail[s, 3 + t, :], win[s, g, HALO - w // 2:2 * HALO - w // 2],
                                                  icnt[s, :], ALU.mult))
                    ch.step(dve.tensor_tensor(tail[:, 3 + t, :], tail[:, 3 + t, :], zp[:, t, HALO:2 * HALO],
                                              ALU.subtract))
                    ch.step(dve.tensor_scalar(tail[:, 3 + t, :], tail[:, 3 + t, :], ps[:, t:t + 1], None, ALU.mult))
                if q == 0:
                    for b, buf in enumerate((gated, outer, zp)):
                        ch.step(dve.tensor_copy(buf[:, :, 0:META], meta3[:, b, :, :]))
                assert ch.n == TAIL_STEPS - 3 * q
                dve.engine_nop().then_inc(tail_made, 1)

            def conv_tail(ch, t):
                dst = tail[:, t, :]
                g = lambda d: gated[:, t, HALO + d:2 * HALO + d]
                ch.step(dve.tensor_scalar(dst, g(-1), cw[:, t, 0:1], None, ALU.mult))
                for d in (0, 1):
                    ch.step(dve.scalar_tensor_tensor(out=dst, in0=g(d), scalar=cw[:, t, d + 1:d + 2], in1=dst,
                                                     op0=ALU.mult, op1=ALU.add))
                return dve.tensor_tensor(dst, dst, outer[:, t, HALO:2 * HALO], ALU.mult)

            norm(0, 0, META)
            rounds(dve, body, flush)

        @block.tensor
        def _(pe):
            pe.wait_ge(consts, 16 * 7)

            def body(r, n, more):
                is_meta = isinstance(r, int) and r == 0
                tiles, rows = (1, META) if is_meta else (NT, P)
                for t in range(tiles):
                    pe.wait_ge(normed, tile(r, t) + 1)
                    for h in range(2):
                        if not is_meta:
                            pe.wait_ge(u_lo_made, 2 * tile(r, t) + h - 1)
                        for k in range(4):
                            ins = pe.transpose(bank[:, 6 + h, P * k:P * k + rows],
                                               xt[0:rows, t, (4 * h + k) * P:(4 * h + k + 1) * P],
                                               ident[0:rows, 0:rows])
                        ins.then_inc(transposed, 1)
                pe.wait_ge(u_lo_made, 2 * tile(r, tiles - 1) + 2)
                for i, j in enumerate(ORDER):
                    before = i - 4 if i >= 4 else i + 8
                    rr = r if i >= 4 else r - 1
                    if not (is_meta and i < 4):
                        if before in act_index:
                            pe.wait_ge(read_act, 9 * rr + act_index[before] + 1)
                        else:
                            pe.wait_ge(gated_made, 3 * rr + before // 3 + 1)
                    for k in range(KD):
                        ins = split_product(pe, bank[:, i % 4, 0:n], (w_hi[:, j, k, :], w_lo[:, j, k, :]),
                                            (u_hi[:, k, 0:n], u_lo[:, k, 0:n]), k == 0, k == KD - 1)
                    ins.then_inc(panel_done, 1)
                for t in range(tiles):
                    s = 1 if is_meta else t % 2
                    if not is_meta:
                        pe.wait_ge(xf_read, tile(r, t))
                    tk = slice(P * t, P * t + rows)
                    for k in range(KD):
                        wf = [w[:, NPAN + 3:NPAN + 5, k, :] for w in (w_hi, w_lo)]
                        ins = split_product(pe, bank[0:rows, 4 + s, 0:FOUR].rearrange("p (a n) -> p a n", a=2),
                                            (u_hi[:, k, tk], u_lo[:, k, tk]), wf, k == 0, k == KD - 1)
                    ins.then_inc(xf_done, 1)

            rounds(pe, body)


def fourier(nc, c):
    TILES = NT * NBLK + 1
    RING = 3
    CH = KCH
    with ExitStack() as ctx:
        sb = lambda n, s, d=F32: ctx.enter_context(nc.sbuf_tensor(n + "_sb", s, d))
        sem = lambda n: ctx.enter_context(nc.semaphore(n))
        xf = sb("xf", [P, TILES, FOUR])
        xf_hi = sb("xf_hi", [P, TILES, FOUR], F32R)
        xf_lo = sb("xf_lo", [P, TILES, FOUR], F32R)
        heads = sb("head_tables", [P, 2, P])
        b_hi = sb("head_hi", [P, 2, P], F32R)
        b_lo = sb("head_lo", [P, 2, P], F32R)
        raw = sb("table_raw", [P, RING, 2, CH])
        t_hi = sb("table_hi", [P, RING, 2, CH], F32R)
        t_lo = sb("table_lo", [P, RING, 2, CH], F32R)
        pq_hi = sb("pq_hi", [P, 4, CH], F32R)
        pq_lo = sb("pq_lo", [P, 4, CH], F32R)
        odd = sb("odd_part", [P, 2, CH])
        fwd = sb("f_forward", [P, 2, CH])
        rev = sb("f_reversed", [P, 2, CH])
        bank = ctx.enter_context(nc.psum_tensor("dft_bank", [P, 8, 512], F32))

        xf_landed, consts = sem("xf_landed"), sem("head_landed")
        t_landed = [sem(f"t_landed{i}") for i in range(RING)]
        xf_hi_made, xf_lo_made = sem("xf_hi_made"), sem("xf_lo_made")
        t_hi_made, t_lo_made, t_used = sem("t_hi_made"), sem("t_lo_made"), sem("t_used")
        pq_hi_made, pq_lo_made = sem("pq_hi_made"), sem("pq_lo_made")
        head_done, odd_made, f_made = sem("head_done"), sem("odd_made"), sem("f_made")
        rev_stored, fwd_stored = sem("rev_stored"), sem("fwd_stored")
        block = ctx.enter_context(nc.Block())

        S1 = list(range(NT * NB1)) + [TILES - 1]
        S2 = list(range(NT * NB1, TILES))
        PER = len(S1)
        USES = [len(range(s, PER, RING)) for s in range(RING)]

        def freed(ch, i):
            if i >= RING:
                return PER * ch + i - RING + 1 + RING
            last = max(j for j in range(PER) if j % RING == i)
            return PER * ch + last - PER + 1 + RING

        def chunks(eng, step, chunk_end):
            with eng.Fori(0, NCH) as ch:
                for i, ti in enumerate(S1):
                    step(ch, i, ti, CH, 0)
                chunk_end(ch, CH, 0)
            for i, ti in enumerate(S2):
                step(NCH, i, ti, K2, 1)
            chunk_end(NCH, K2, 1)

        def rows_of(ti):
            return META if ti == TILES - 1 else P

        @block.sync
        def _(sp):
            for q in range(4):
                t = slice(5 * q, 5 * q + 5)
                sp.dma_start(xf[:, t, :], c["xf"][t, :, :].rearrange("t p n -> p t n")).then_inc(xf_landed, 16)
            sp.dma_start(xf[0:META, TILES - 1, :], c["xf"][TILES - 1, 0:META, :]).then_inc(xf_landed, 16)
            sp.dma_start(heads[:, :, :], c["head_tables"]).then_inc(consts, 16)

            def step(ch, i, ti, n, seq):
                sp.wait_ge(t_lo_made, freed(ch, i))
                r = rows_of(ti)
                if seq == 0:
                    src = c["table1"][bass.ds(ch, 1), i, 0:r, :].rearrange("a p n -> p (a n)")
                    dst = raw[0:r, i % RING, :, :].rearrange("p a n -> p (a n)")
                else:
                    src = c["table2"][i, 0:r, :].rearrange("p (a n) -> p a n", a=2)
                    dst = raw[0:r, i % RING, :, 0:n]
                sp.dma_start(dst, src).then_inc(t_landed[i % RING], 16)

            def chunk_end(ch, n, seq):
                sp.wait_ge(f_made, 2 * ch + 3)
                skip = 0 if seq == 0 else META - 1
                k0, r0 = (CH * ch + 1, CH * (0 - ch) + L1 - CH) if seq == 0 else (SEQ + META, SEQ + L2 - n)
                dst = c["mixT"][2 * CONV:D, :].rearrange("(m p) n -> p m n", p=P)
                sp.dma_start(dst[:, :, bass.ds(r0, n)], rev[:, :, 0:n]).then_inc(rev_stored, 16)
                sp.wait_ge(rev_stored, 16 * ch + 16)
                sp.dma_start(dst[:, :, bass.ds(k0, n - skip)], fwd[:, :, skip:n]).then_inc(fwd_stored, 16)

            sp.nop().then_inc(fwd_stored, 16)
            chunks(sp, step, chunk_end)
            sp.wait_ge(fwd_stored, 16 * (NCH + 2))


        @block.scalar
        def _(act):
            for q in range(4):
                act.wait_ge(xf_landed, 16 * 5)
                t = slice(5 * q, 5 * q + 5)
                act.activation(xf_hi[:, t, :], xf[:, t, :], ACT.Copy).then_inc(xf_hi_made, 1)
            act.activation(xf_hi[0:META, TILES - 1, :], xf[0:META, TILES - 1, :], ACT.Copy).then_inc(xf_hi_made, 1)
            act.wait_ge(consts, 16)
            act.activation(b_hi[:, :, :], heads[:, :, :], ACT.Copy).then_inc(xf_hi_made, 1)

            def step(ch, i, ti, n, seq):
                s, r = i % RING, rows_of(ti)
                act.wait_ge(t_landed[s], 16 * (USES[s] * ch + i // RING + 1))
                act.wait_ge(t_used, freed(ch, i))
                act.activation(t_hi[0:r, s, :, 0:n], raw[0:r, s, :, 0:n], ACT.Copy).then_inc(t_hi_made, 1)

            def chunk_end(ch, n, seq):
                act.wait_ge(t_used, (PER * ch + PER if seq == 0 else PER * NCH + len(S2)) + RING)
                for q in range(4):
                    act.activation(pq_hi[:, q, 0:n], bank[:, q, 0:n], ACT.Copy).then_inc(pq_hi_made, 1)
                act.wait_ge(f_made, 2 * ch + 1)
                for m in range(2):
                    act.wait_ge(head_done, 4 * ch + 2 * m + 2)
                    act.activation(odd[:, m, 0:n], bank[:, 6 + m, 0:n], ACT.Copy).then_inc(odd_made, 1)

            chunks(act, step, chunk_end)


        @block.vector
        def _(dve):
            dve.nop().then_inc(t_lo_made, RING)
            dve.nop().then_inc(pq_lo_made, 1)
            dve.nop().then_inc(f_made, 1)
            for q in range(4):
                dve.wait_ge(xf_hi_made, q + 1)
                t = slice(5 * q, 5 * q + 5)
                dve.tensor_tensor(xf_lo[:, t, :], xf[:, t, :], xf_hi[:, t, :].bitcast(F32), ALU.subtract)\
                    .then_inc(xf_lo_made, 1)
            dve.wait_ge(xf_hi_made, 5)
            dve.tensor_tensor(xf_lo[0:META, TILES - 1, :], xf[0:META, TILES - 1, :],
                              xf_hi[0:META, TILES - 1, :].bitcast(F32), ALU.subtract).then_inc(xf_lo_made, 1)
            dve.wait_ge(xf_hi_made, 6)
            dve.tensor_tensor(b_lo[:, :, :], heads[:, :, :], b_hi[:, :, :].bitcast(F32), ALU.subtract)\
                .then_inc(xf_lo_made, 1)

            def step(ch, i, ti, n, seq):
                s, r = i % RING, rows_of(ti)
                dve.wait_ge(t_hi_made, PER * ch + i + 1)
                dve.tensor_tensor(t_lo[0:r, s, :, 0:n], raw[0:r, s, :, 0:n], t_hi[0:r, s, :, 0:n].bitcast(F32),
                                  ALU.subtract).then_inc(t_lo_made, 1)

            def chunk_end(ch, n, seq):
                for q in range(4):
                    dve.wait_ge(pq_hi_made, 4 * ch + q + 1)
                    dve.tensor_tensor(pq_lo[:, q, 0:n], bank[:, q, 0:n], pq_hi[:, q, 0:n].bitcast(F32),
                                      ALU.subtract).then_inc(pq_lo_made, 1)
                dve.wait_ge(fwd_stored, 16 * ch + 16)
                for m in range(2):
                    dve.wait_ge(odd_made, 2 * ch + m + 1)
                    dve.tensor_tensor(rev[:, m, 0:n][:, ::-1], bank[:, 4 + m, 0:n], odd[:, m, 0:n], ALU.add)
                    dve.tensor_tensor(fwd[:, m, 0:n], bank[:, 4 + m, 0:n], odd[:, m, 0:n], ALU.subtract)\
                        .then_inc(f_made, 1)

            chunks(dve, step, chunk_end)


        @block.tensor
        def _(pe):
            pe.nop().then_inc(t_used, RING)
            pe.wait_ge(xf_lo_made, 6)

            def step(ch, i, ti, n, seq):
                s, r = i % RING, rows_of(ti)
                pe.wait_ge(t_lo_made, PER * ch + i + 1 + RING)
                if i == 0:
                    pe.wait_ge(pq_lo_made, 4 * ch + 1)
                last = ti == TILES - 1
                for m in range(2):
                    w = [x[0:r, ti, P * m:P * m + P] for x in (xf_hi, xf_lo)]
                    for a in range(2):
                        ins = split_product(pe, bank[:, 2 * m + a, 0:n], w,
                                            [t[0:r, s, a, 0:n] for t in (t_hi, t_lo)], i == 0, last)
                ins.then_inc(t_used, 1)

            def chunk_end(ch, n, seq):
                for m in range(2):
                    for a in range(2):
                        pe.wait_ge(pq_lo_made, 4 * ch + 2 * m + a + 2)
                        split_product(pe, bank[:, 4 + 2 * a + m, 0:n], (b_hi[:, a, :], b_lo[:, a, :]),
                                      (pq_hi[:, 2 * m + a, 0:n], pq_lo[:, 2 * m + a, 0:n]), True, True)\
                            .then_inc(head_done, 1)

            chunks(pe, step, chunk_end)



def finish(nc, c, ident, half, eps):
    BANKS = (4, 5, 6, 7, 0, 1, 2, 3)
    RING = 4
    G0, D0 = KD, KD + 2 * MF
    PER = D0 + MF
    GROUP_OF = (0, 0, 0, 1, 1, 1, 2, 2)
    FIRST, LAST = (0, 3, 6), (2, 5, 7)
    assert G0 % RING == 0 and D0 % RING == 0
    FIRST_TURN = (*range(1, 8), 0)
    USES = [len(range(s, PER, RING)) for s in range(RING)]
    MIX_STEP = {2 + 2 * k: k for k in range(KD)}
    with ExitStack() as ctx:
        sb = lambda n, s, d=F32: ctx.enter_context(nc.sbuf_tensor(n + "_sb", s, d))
        sem = lambda n: ctx.enter_context(nc.semaphore(n))
        w_raw = sb("w_raw", [P, RING, D])
        w_hi = sb("w_panel_hi", [P, RING, D], F32R)
        w_lo = sb("w_panel_lo", [P, RING, D], F32R)
        v_hi = sb("v_hi", [P, KD, T], F32R)
        v_lo = sb("v_lo", [P, KD, T], F32R)
        a_hi = sb("act_hi", [P, MF, T], F32R)
        a_lo = sb("act_lo", [P, MF, T], F32R)
        h = sb("h", [P, NT, D])
        stage = sb("stage", [P, 2, D])
        mx = sb("mix_raw", [P, 2, T])
        squares = sb("mix_squares", [P, 3, T])
        g2 = squares[:, 0:2, :].rearrange("p a n -> p (a n)")
        ms_now = sb("mix_mean_sq", [P, 12])
        width = sb("group_means", [P, 3])
        gf = sb("final_rows", [P, D])
        mg = sb("mix_g_cols", [P, KD])
        rs_now = sb("rs_now", [P, 12])
        msq = sb("h_mean_sq", [P, NT])
        ms = sb("h_ms", [P, NT])
        rstd = sb("h_rstd", [P, NT])
        bank = ctx.enter_context(nc.psum_tensor("fin_bank", [P, 8, 512], F32))

        consts = sem("fin_consts")
        w_landed = [sem(f"w_landed{i}") for i in range(RING)]
        w_hi_made, w_lo_made, w_used = sem("w_hi_made"), sem("w_lo_made"), sem("w_used")
        h_landed = [sem(f"h_landed{i}") for i in range(NT)]
        m_landed = [sem(f"mix_landed{i}") for i in range(2)]
        m_hi_made, m_lo_made, squares_step, m_used = sem("m_hi_made"), sem("m_lo_made"), sem("squares_step"), sem("m_used")
        g2_landed = sem("g2_landed")
        stat_done, ms_made, rs_made = sem("stat_done"), sem("mix_ms_made"), sem("mix_rs_made")
        proj_done, proj_read = sem("proj_done"), sem("proj_read")
        squared, rstd_step, rstd_made = sem("h_squared"), sem("h_rstd_step"), sem("h_rstd_made")
        v_made, transposed = sem("v_made"), sem("v_transposed")
        v_hi_made, v_lo_made = sem("v_hi_made"), sem("v_lo_made")
        silu_made, glu_made = sem("silu_made"), sem("glu_made")
        a_hi_made, a_lo_made = sem("a_hi_made"), sem("a_lo_made")
        down_done, down_read, y_made = sem("down_done"), sem("down_read"), sem("y_made")
        y_stored = [sem(f"y_stored{i}") for i in range(2)]
        block = ctx.enter_context(nc.Block())

        def blocks(eng, body):
            with eng.Fori(0, NBLK - 1) as b:
                body(b, True)
            body(NBLK - 1, False)

        def freed(b, q):
            if not isinstance(q, int) or q >= RING:
                return PER * b + q + 1
            return PER * b + max(j for j in range(PER) if j % RING == q) - PER + 1 + RING

        START = (2, 3, 0, 1)

        def order(q):
            return START.index(q) if isinstance(q, int) and q < RING else q

        def freed_raw(b, q):
            if isinstance(q, int) and RING <= q < 2 * RING:
                return PER * b + order(q - RING) + 1 + RING
            return freed(b, q)

        def stream(b, q, more, split):
            if q + RING < PER:
                split(b, q + RING, (q + RING) % RING)
            elif more:
                n = START[q + RING - PER]
                split(b + 1, n, n)

        @block.sync
        def _(sp):
            for dst, name in ((gf[:, :], "final_rows"), (mg[:, :], "mix_g_cols"),
                              (width[:, :], "group_means")):
                sp.dma_start(dst, c[name]).then_inc(consts, 16)

            def mix_load(b, k):
                sp.wait_ge(m_used, KD * b + k + 1)
                sp.dma_start(mx[:, k % 2, :], c["mixT"][P * k:P * k + P, bass.ds(T * b + META, T)])\
                    .then_inc(m_landed[k % 2], 16)

            def h_load(b, t):
                sp.dma_start(h[:, t, :], c["x"][bass.ds(T * b + P * t, P), :]).then_inc(h_landed[t], 16)

            def panel(b, q, s):
                sp.wait_ge(w_lo_made, freed_raw(b, q))
                sp.dma_start(w_raw[:, s, :], c["w_panels"][bass.ds(q, 1), :, :].rearrange("a p n -> p (a n)"))\
                    .then_inc(w_landed[s], 16)

            def body(b, more):
                sp.wait_ge(stat_done, b + 1)
                sp.dma_start(g2, c["norm2_rows"]).then_inc(g2_landed, 16)
                for q in range(RING, KD):
                    stream(b, q, more, panel)
                with sp.Fori(0, MF // 2) as i:
                    for s in range(RING):
                        panel(b, RING * i + G0 + RING + s, s)
                for q in range(D0, PER):
                    stream(b, q, more, panel)
                    if more and q - D0 in MIX_STEP:
                        mix_load(b + 1, MIX_STEP[q - D0])
                if more:
                    for q in START[:3]:
                        stream(b + 1, q, more, panel)
                for t in range(NT):
                    if more and t == 2:
                        stream(b + 1, START[3], more, panel)
                    sp.wait_ge(y_made, NT * b + t + 1)
                    sp.dma_start(c["out"][bass.ds(T * b + P * t, P), :], stage[:, t % 2, :])\
                        .then_inc(y_stored[t % 2], 16)
                    if more:
                        h_load(b + 1, t)

            for s in y_stored:
                sp.nop().then_inc(s, 16)
            for k in range(2):
                mix_load(0, k)
            for q in START:
                panel(0, q, q)
            for k in range(2, KD):
                mix_load(0, k)
            for q in range(RING):
                stream(0, q, True, panel)
            for t in range(NT):
                h_load(0, t)
            blocks(sp, body)
            for s in y_stored:
                sp.wait_ge(s, 16 * (1 + 2 * NBLK))

        @block.gpsimd
        def _(pool):
            pool.nop().then_inc(m_used, 2)
            pool.wait_ge(consts, 48)

            def mix_square(b, k):
                g, raw = GROUP_OF[k], mx[:, k % 2, :]
                step = KD * b + k
                pool.wait_ge(m_lo_made, KD * b + k + 3)
                if k in FIRST:
                    if k == 0 and not (isinstance(b, int) and b == 0):
                        pool.wait_ge(v_made, NT * b)
                    pool.tensor_tensor(squares[:, g, :], raw, raw, ALU.mult).then_inc(m_used, 1)
                else:
                    pool.tensor_tensor(raw, raw, raw, ALU.mult).then_inc(squares_step, 1)
                    pool.wait_ge(squares_step, (KD - 3) * b + k - g)
                    pool.wait_ge(m_used, KD * b + k + 2)
                    pool.tensor_tensor(squares[:, g, :], squares[:, g, :], raw, ALU.add).then_inc(m_used, 1)

            def group_rstd(b):
                pool.wait_ge(ms_made, b + 1)
                pool.tensor_tensor(rs_now[:, :], ms_now[:, :], half[:, 0:12], ALU.pow).then_inc(rs_made, 1)

            def tile_rstd(b, n):
                t = n % NT
                pool.wait_ge(squared, 2 * NT * b + n + 1)
                pool.tensor_tensor(ms[:, t:t + 1], msq[:, t:t + 1], eps[:, :], ALU.add).then_inc(rstd_step, 1)
                pool.wait_ge(rstd_step, 2 * NT * b + n + 1)
                pool.tensor_tensor(rstd[:, t:t + 1], ms[:, t:t + 1], half[:, 0:1], ALU.pow).then_inc(rstd_made, 1)

            def body(b, more):
                for t in range(NT):
                    tile_rstd(b, t)
                if more:
                    for k in range(KD):
                        mix_square(b + 1, k)
                for t in range(NT):
                    tile_rstd(b, NT + t)
                if more:
                    group_rstd(b + 1)

            for k in range(KD):
                mix_square(0, k)
            group_rstd(0)
            blocks(pool, body)

        @block.scalar
        def _(act):
            act.wait_ge(consts, 48)

            def mix_split(b, k):
                act.wait_ge(m_landed[k % 2], 16 * (KD // 2 * b + k // 2 + 1))
                act.activation(v_hi[:, k, :], mx[:, k % 2, :], ACT.Copy, scale=mg[:, k:k + 1]).then_inc(m_hi_made, 1)

            def split(b, q, s, turn=None):
                act.wait_ge(w_landed[s], 16 * (USES[s] * b + (q // RING + 1 if turn is None else turn + 1)))
                act.wait_ge(w_used, freed(b, q))
                act.activation(w_hi[:, s, :], w_raw[:, s, :], ACT.Copy).then_inc(w_hi_made, 1)

            def square(b, n):
                t = n % NT
                act.wait_ge(squared, 2 * NT * b + n)
                act.activation(mx.rearrange("p s n -> p (s n)"), h[:, t, :], ACT.Square, scale=D ** -0.5,
                               accum_out=msq[:, t:t + 1]).then_inc(squared, 1)

            def v_split(b, t):
                for g in range(2):
                    act.wait_ge(transposed, 2 * NT * b + 2 * t + g + 1)
                    act.activation(v_hi[:, 4 * g:4 * g + 4, P * t:P * t + P],
                                   bank[:, BANKS[2 * t + g], :].rearrange("p (k n) -> p k n", k=4), ACT.Copy)\
                        .then_inc(v_hi_made, 1)

            def body(b, more):
                for q in range(KD - 3):
                    stream(b, q, more, split)
                for t in range(NT):
                    act.wait_ge(proj_read, 24 * b + 16 + 2 * t + 2)
                    square(b, t)
                    if t == 2:
                        v_split(b, 0)
                for t in range(1, NT):
                    v_split(b, t)
                for q in range(KD - 3, KD):
                    stream(b, q, more, split)
                with act.Fori(0, MF // 2) as i:
                    for p in range(2):
                        act.wait_ge(w_used, PER * b + RING * i + 2 * p + G0 + 1 + RING)
                        act.wait_ge(a_lo_made, MF * b + 2 * i + p + 1)
                        act.activation(stage[:, p, 0:T], bank[:, 2 * p, :], ACT.Silu).then_inc(silu_made, 1)
                        for s in (2 * p, 2 * p + 1):
                            split(b, RING * i + G0 + RING + s, s, i + G0 // RING + 1)
                        act.wait_ge(glu_made, MF * b + 2 * i + p + 3)
                        act.activation(a_hi[:, bass.ds(2 * i + p, 1), :].rearrange("p a n -> p (a n)"),
                                       stage[:, p, 0:T], ACT.Copy).then_inc(a_hi_made, 1)
                for q in range(D0, PER - 1):
                    stream(b, q, more, split)
                    if more and q - D0 in MIX_STEP:
                        mix_split(b + 1, MIX_STEP[q - D0])
                for t in range(NT):
                    act.wait_ge(down_read, 8 * b + 8 + 2 * t + 2)
                    if t == 0 and more:
                        act.wait_ge(m_used, KD * b + 2 * KD + 2)
                    square(b, NT + t)
                    if t == 1:
                        stream(b, PER - 1, more, split)

            mix_split(0, 0)
            for q in START:
                split(0, q, q)
            for k in range(1, KD):
                mix_split(0, k)
            blocks(act, body)

        @block.vector
        def _(dve):
            dve.nop().then_inc(w_lo_made, RING)
            dve.nop().then_inc(m_lo_made, 2)
            dve.nop().then_inc(glu_made, 2)
            dve.nop().then_inc(a_lo_made, 2)
            dve.nop().then_inc(down_read, 8)
            dve.wait_ge(consts, 48)

            def mix_split(b, k):
                dve.wait_ge(m_hi_made, KD * b + k + 1)
                dve.scalar_tensor_tensor(out=v_lo[:, k, :], in0=mx[:, k % 2, :], scalar=mg[:, k:k + 1],
                                         in1=v_hi[:, k, :].bitcast(F32), op0=ALU.mult, op1=ALU.subtract)\
                    .then_inc(m_lo_made, 1)

            def split(b, q, s):
                dve.wait_ge(w_hi_made, PER * b + order(q) + 1)
                dve.tensor_tensor(w_lo[:, s, :], w_raw[:, s, :], w_hi[:, s, :].bitcast(F32), ALU.subtract)\
                    .then_inc(w_lo_made, 1)

            def proj_add(b, g, j):
                t, n = j // 2, j % 2
                if j < 7:
                    dve.wait_ge(proj_done, 21 * b + 7 * g + j + 1)
                else:
                    dve.wait_ge(w_used, PER * b + LAST[g] + 1 + RING)
                part = h[:, t, 512 * n:512 * n + 512]
                if g == 0:
                    dve.wait_ge(h_landed[t], 16 * b + 16)
                else:
                    dve.wait_ge(proj_read, 24 * b + 8 * g - 8 + j + 1)
                dve.scalar_tensor_tensor(out=part, in0=bank[:, BANKS[j], :], scalar=rs_now[:, 4 * g + t:4 * g + t + 1],
                                         in1=part, op0=ALU.mult, op1=ALU.add).then_inc(proj_read, 1)

            def v_norm(b, t):
                dve.wait_ge(rstd_made, 2 * NT * b + t + 1)
                if t < 2:
                    dve.wait_ge(y_stored[t], 16 * (2 * b + 1))
                else:
                    dve.wait_ge(transposed, 2 * NT * b + 2 * t - 2)
                if t == 0:
                    dve.wait_ge(g2_landed, 16 * b + 16)
                dve.scalar_tensor_tensor(out=stage[:, t % 2, :], in0=h[:, t, :], scalar=rstd[:, t:t + 1], in1=g2,
                                         op0=ALU.mult, op1=ALU.mult).then_inc(v_made, 1)

            def v_split(b, t):
                for g in range(2):
                    dve.wait_ge(v_hi_made, 2 * NT * b + 2 * t + g + 1)
                    part = lambda v: v[:, 4 * g:4 * g + 4, P * t:P * t + P]
                    dve.tensor_tensor(part(v_lo), bank[:, BANKS[2 * t + g], :].rearrange("p (k n) -> p k n", k=4),
                                      part(v_hi).bitcast(F32), ALU.subtract).then_inc(v_lo_made, 1)

            def mix_means(b):
                dve.wait_ge(stat_done, b + 1)
                dve.tensor_scalar(ms_now[:, :], bank[:, BANKS[0], 0:12], EPS, None, ALU.add).then_inc(ms_made, 1)

            def y_norm(b, t):
                dve.wait_ge(rstd_made, 2 * NT * b + NT + t + 1)
                if t >= 2:
                    dve.wait_ge(y_stored[t % 2], 16 * (2 * b + 2))
                dve.scalar_tensor_tensor(out=stage[:, t % 2, :], in0=h[:, t, :], scalar=rstd[:, t:t + 1],
                                         in1=gf[:, :], op0=ALU.mult, op1=ALU.mult).then_inc(y_made, 1)

            def body(b, more):
                dve.wait_ge(rs_made, b + 1)
                for q in range(KD - 2):
                    if q in LAST[:2]:
                        for j in range(8):
                            proj_add(b, GROUP_OF[q], j)
                    if q < KD - 3:
                        stream(b, q, more, split)
                proj_tile = lambda t: [proj_add(b, 2, j) for j in (2 * t, 2 * t + 1)]
                proj_tile(0)
                proj_tile(1)
                v_norm(b, 0)
                proj_tile(2)
                v_norm(b, 1)
                proj_add(b, 2, 6)
                v_norm(b, 2)
                proj_add(b, 2, 7)
                v_split(b, 0)
                v_norm(b, 3)
                v_split(b, 1)
                v_split(b, 2)
                v_split(b, 3)
                for q in range(KD - 3, KD):
                    stream(b, q, more, split)
                with dve.Fori(0, MF // 2) as i:
                    for p in range(2):
                        m = 2 * i + p
                        split(b, RING * i + G0 + RING + 2 * p, 2 * p)
                        dve.wait_ge(silu_made, MF * b + m + 1)
                        dve.wait_ge(w_used, PER * b + RING * i + 2 * p + G0 + 2 + RING)
                        dve.tensor_tensor(stage[:, p, 0:T], bank[:, 2 * p + 1, :], stage[:, p, 0:T], ALU.mult)\
                            .then_inc(glu_made, 1)
                        split(b, RING * i + G0 + RING + 2 * p + 1, 2 * p + 1)
                        dve.wait_ge(a_hi_made, MF * b + m + 1)
                        at = lambda a: a[:, bass.ds(m, 1), :].rearrange("p a n -> p (a n)")
                        dve.tensor_tensor(at(a_lo), stage[:, p, 0:T], at(a_hi).bitcast(F32), ALU.subtract)\
                            .then_inc(a_lo_made, 1)
                for q in range(D0, PER - 1):
                    stream(b, q, more, split)
                    if more and q - D0 in MIX_STEP:
                        mix_split(b + 1, MIX_STEP[q - D0])
                for t in range(NT):
                    for j in (2 * t, 2 * t + 1):
                        if j < 7:
                            dve.wait_ge(down_done, 7 * b + j + 1)
                        else:
                            dve.wait_ge(w_used, PER * b + PER + RING)
                        part = h[:, t, 512 * (j % 2):512 * (j % 2) + 512]
                        dve.tensor_tensor(part, bank[:, BANKS[j], :], part, ALU.add).then_inc(down_read, 1)
                    if t == 2 and more:
                        mix_means(b + 1)
                    if t and not more:
                        y_norm(b, t - 1)
                if more:
                    y_norm(b, 0)
                    stream(b, PER - 1, more, split)
                    y_norm(b, 1)
                    y_norm(b, 2)
                y_norm(b, NT - 1)

            mix_split(0, 0)
            for q in START:
                split(0, q, q)
            for k in range(1, KD):
                mix_split(0, k)
            mix_means(0)
            blocks(dve, body)

        @block.tensor
        def _(pe):
            pe.nop().then_inc(w_used, RING)

            def product(b, q, src, k, j, first, last):
                t, n, s = j // 2, j % 2, q % RING
                return split_product(pe, bank[:, BANKS[j], :], [x[:, k, P * t:P * t + P] for x in src],
                                     [w[:, s, 512 * n:512 * n + 512] for w in (w_hi, w_lo)], first, last)

            def statistics(b):
                pe.wait_ge(down_read, 8 * b + 1)
                pe.wait_ge(m_used, KD * b + KD + 2)
                for g in range(3):
                    for t in range(NT):
                        ins = pe.matmul(bank[:, BANKS[0], 4 * g + t:4 * g + t + 1], squares[:, g, P * t:P * t + P],
                                        width[:, g:g + 1], start=(g == 0 and t == 0), stop=True,
                                        skip_group_check=True)
                ins.then_inc(stat_done, 1)

            def transpose(b, t):
                pe.wait_ge(v_made, NT * b + t + 1)
                for g in range(2):
                    for k in range(4):
                        ins = pe.transpose(bank[:, BANKS[2 * t + g], P * k:P * k + P],
                                           stage[:, t % 2, (4 * g + k) * P:(4 * g + k + 1) * P], ident[:, :])
                    ins.then_inc(transposed, 1)

            def body(b, more):
                statistics(b)
                for k in range(KD - 2):
                    g = GROUP_OF[k]
                    pe.wait_ge(m_lo_made, KD * b + k + 3)
                    pe.wait_ge(w_lo_made, PER * b + max(order(k), k) + 1 + RING)
                    for j in FIRST_TURN if k == 0 else range(8):
                        if k == 0:
                            pe.wait_ge(down_read, 8 * b + j + 1)
                            if j == 0:
                                pe.wait_ge(ms_made, b + 1)
                        elif k in FIRST:
                            pe.wait_ge(proj_read, 24 * b + 8 * g - 8 + j + 1)
                        ins = product(b, k, (v_hi, v_lo), k, j, k in FIRST, k in LAST)
                        if k in LAST and j < 7:
                            ins.then_inc(proj_done, 1)
                    ins.then_inc(w_used, 1)
                pe.wait_ge(m_lo_made, KD * b + KD + 2)
                pe.wait_ge(w_lo_made, PER * b + KD + RING)
                for j in range(8):
                    pe.wait_ge(proj_read, 24 * b + 8 + j + 1)
                    for k in (KD - 2, KD - 1):
                        ins = product(b, k, (v_hi, v_lo), k, j, k == KD - 2, k == KD - 1)
                        if j == 7:
                            ins.then_inc(w_used, 1)
                    if j < 7:
                        ins.then_inc(proj_done, 1)
                    if j == 5:
                        transpose(b, 0)
                for t in range(1, NT):
                    transpose(b, t)
                with pe.Fori(0, MF // 2) as i:
                    pe.wait_ge(v_lo_made, 2 * NT * (b + 1))
                    for p in range(2):
                        pe.wait_ge(glu_made, MF * b + 2 * i + p + 1)
                        for s in (2 * p, 2 * p + 1):
                            pe.wait_ge(w_lo_made, PER * b + RING * i + G0 + s + 1 + RING)
                            for k in range(KD):
                                ins = split_product(pe, bank[:, s, :],
                                                    [w[:, s, P * k:P * k + P] for w in (w_hi, w_lo)],
                                                    (v_hi[:, k, :], v_lo[:, k, :]), k == 0, k == KD - 1)
                            ins.then_inc(w_used, 1)
                for k in range(MF):
                    pe.wait_ge(a_lo_made, MF * b + k + 3)
                    pe.wait_ge(w_lo_made, PER * b + D0 + k + 1 + RING)
                    for j in range(8):
                        if k == 0 and BANKS[j] < 4:
                            pe.wait_ge(glu_made, MF * b + MF + 1 + BANKS[j] // 2)
                        ins = product(b, D0 + k, (a_hi, a_lo), k, j, k == 0, k == MF - 1)
                        if k == MF - 1 and j < 7:
                            ins.then_inc(down_done, 1)
                    ins.then_inc(w_used, 1)

            blocks(pe, body)


def build(nc, c):
    with ExitStack() as ctx:
        ident = ctx.enter_context(nc.sbuf_tensor("ident_sb", [P, P], F32))
        half = ctx.enter_context(nc.sbuf_tensor("minus_half_sb", [P, 12], F32))
        eps = ctx.enter_context(nc.sbuf_tensor("eps_sb", [P, 1], F32))
        with nc.sbuf_tensor("w_in_hi", [P, NPAN + 5, KD, P], F32R) as w_hi, \
                nc.sbuf_tensor("w_in_lo", [P, NPAN + 5, KD, P], F32R) as w_lo:
            prepare(nc, c, w_hi, w_lo)
            project(nc, c, w_hi, w_lo, ident, half, eps)
        fourier(nc, c)
        finish(nc, c, ident, half, eps)


def dft_tables(length, rows, freqs):
    turns = (rows[:, None] * freqs[None, :]) % length * (2 * np.pi / length)
    return (np.stack([np.cos(turns), np.sin(turns)], axis=1) / np.sqrt(length)).astype(np.float32)


def constants():
    k = {"ident": np.eye(P, dtype=np.float32), "minus_half": np.full((P, 12), -0.5, np.float32),
         "group_means": np.tile(np.float32([1 / CONV, 1 / CONV, 1 / FOUR]), (P, 1)), "eps": np.full((P, 1), EPS, np.float32)}
    back = np.arange(8)[::-1]
    k["inv_counts"] = np.repeat(np.stack([1.0 / (np.minimum(w - 1 - w // 2, back) + w // 2 + 1) for w in WINDOWS]),
                                32, axis=0).astype(np.float32)
    dims = np.arange(HD)
    head = dft_tables(HD, dims, dims)
    tables = np.zeros((P, 2, P), np.float32)
    for n in range(P // HD):
        tables[HD * n:HD * n + HD, :, HD * n:HD * n + HD] = head
    k["head_tables"] = tables
    for name, length, freqs, chunks in (("table1", L1, NCH * KCH, NCH), ("table2", L2, K2, 1)):
        at = np.arange(META, length)
        width = freqs // chunks
        out = np.zeros((chunks, (length - META) // P + 1, P, 2 * width), np.float32)
        for n in range(chunks):
            f = np.arange(1 + n * width, 1 + (n + 1) * width)
            out[n, :-1] = dft_tables(length, at, f).reshape(-1, P, 2 * width)
            out[n, -1, 0:META] = dft_tables(length, np.arange(META), f).reshape(META, 2 * width)
        k[name] = out if chunks > 1 else out[0]
    return k


def kernel(x_prompt, x_sample, meta_tokens, norm1_g, w_in, conv_w, pool_w, pool_scale, mix_g, w_out, norm2_g,
           w_gate_up, w_down, final_g):
    import concourse.bacc as bacc
    from concourse.bass_utils import run_bass_kernel_spmd

    asc = np.ascontiguousarray
    x_prompt, x_sample, w_in, w_out, w_gu, w_down = (
        np.asarray(a) for a in (x_prompt, x_sample, w_in[0], w_out[0], w_gate_up[0], w_down[0]))
    arrays = constants()
    arrays["x"] = np.concatenate([x_prompt[0], x_sample[0]])
    arrays["meta"] = np.asarray(meta_tokens)
    for name, g in (("norm1_rows", norm1_g[0]), ("norm2_rows", norm2_g[0]), ("final_rows", final_g)):
        arrays[name] = asc(np.broadcast_to(np.asarray(g), (P, D)))

    def column_panels(w):
        return asc(w.reshape(KD, P, -1, P).transpose(2, 1, 0, 3)).reshape(-1, P, D)

    four = column_panels(w_in[:, 3 * CONV + CONV:])
    arrays["w_in_panels"] = np.concatenate([column_panels(w_in[:, 0:3 * CONV]), four])
    arrays["w_pool_T"] = asc(w_in[:, 3 * CONV:4 * CONV].T).reshape(4, GROUP, D)
    arrays["pool_w"] = asc(np.asarray(pool_w[0]))
    arrays["conv_cols"] = asc(np.asarray(conv_w[0]).reshape(3, 3, P).transpose(2, 1, 0))

    def pool_order(a):
        return a.reshape(4, 3, 32, -1).transpose(1, 0, 2, 3).reshape(CONV, -1)

    def mixed(a):
        a = np.asarray(a).reshape(D, -1)
        return np.concatenate([a[0:CONV], pool_order(a[CONV:2 * CONV]), a[2 * CONV:]])

    arrays["pool_scale_cols"] = asc(pool_order(np.asarray(pool_scale[0])).reshape(3, P).T)
    arrays["mix_g_cols"] = asc(mixed(mix_g[0]).reshape(KD, P).T)
    gate, up = column_panels(w_gu[:, 0:DFF]), column_panels(w_gu[:, DFF:])
    arrays["w_panels"] = np.concatenate([mixed(w_out).reshape(KD, P, D),
                                         np.stack([gate, up], axis=1).reshape(-1, P, D),
                                         w_down.reshape(MF, P, D)])

    nc = bacc.Bacc("TRN2", target_bir_lowering=False, num_devices=1)
    c = {n: nc.dram_tensor(n, list(a.shape), F32, kind="ExternalInput").ap() for n, a in arrays.items()}
    c["mixT"] = nc.dram_tensor("mixT", [D, META + SEQ + DEC], F32).ap()
    c["xf"] = nc.dram_tensor("xf", [NT * NBLK + 1, P, FOUR], F32).ap()
    c["out"] = nc.dram_tensor("out", [SEQ + DEC, D], F32, kind="ExternalOutput").ap()
    build(nc, c)
    r = run_bass_kernel_spmd(nc, [arrays], core_ids=[0])
    out = r.results[0]["out"]
    return out[None, 0:SEQ], out[None, SEQ:]
```

```python
from contextlib import ExitStack

import numpy as np

import concourse.bass as bass
from concourse import mybir
from concourse.alu_op_type import AluOpType as ALU

ACT = mybir.ActivationFunctionType
F32 = mybir.dt.float32
F32R = mybir.dt.float32r

P = 128
D = 1024
KD = D // P
META = 16
SEQ, DEC = 2048, 512
L1, L2 = META + SEQ, META + DEC
T = 512
NT = T // P
NB1 = SEQ // T
NBLK = (SEQ + DEC) // T
CONV = 3 * D // 8
HALO = 8
GROUP = CONV // 4
FOUR = D - 2 * CONV
HD = FOUR // 4
DFF = -(-8 * D // (3 * 256)) * 256
MF = DFF // P
EPS = 1e-6
NPAN = 3 * CONV // P
KCH, NCH = 344, 3
K2 = L2 // 2
WINDOWS = (2, 4, 8, 16)
RING = 4
G0, D0 = KD, KD + 2 * MF
PER = D0 + MF
USES = [len(range(s, PER, RING)) for s in range(RING)]
START = (2, 3, 0, 1)
GROUP_OF = (0, 0, 0, 1, 1, 1, 2, 2)
FIRST, LAST = (0, 3, 6), (2, 5, 7)
assert NCH * KCH == L1 // 2 and DFF % 256 == 0 and G0 % RING == 0 and D0 % RING == 0 and PER % RING == 2


def split_product(pe, out, w, x, first, last):
    pe.matmul(out, w[0], x[0], start=first, stop=False, skip_group_check=True)
    pe.matmul(out, w[0], x[1], start=False, stop=False, skip_group_check=True)
    return pe.matmul(out, w[1], x[0], start=False, stop=last, skip_group_check=True)


class Chain:

    def __init__(self, eng, sem, base=0):
        self.eng, self.sem, self.base, self.n = eng, sem, base, 0

    def step(self, ins):
        self.n += 1
        ins.then_inc(self.sem, 1)
        self.eng.wait_ge(self.sem, self.base + self.n)


def project(nc, c, ident, half, eps, tail, tail_stored):
    W = META + T
    with ExitStack() as ctx:
        sb = lambda n, s, d=F32: ctx.enter_context(nc.sbuf_tensor(n + "_sb", s, d))
        sem = lambda n: ctx.enter_context(nc.semaphore(n))
        w_hi = sb("w_in_hi", [P, NPAN + 5, KD, P], F32R)
        w_lo = sb("w_in_lo", [P, NPAN + 5, KD, P], F32R)
        u_hi = sb("u_hi", [P, KD, T], F32R)
        u_lo = sb("u_lo", [P, KD, T], F32R)
        um_hi = sb("u_meta_hi", [P, KD, META], F32R)
        um_lo = sb("u_meta_lo", [P, KD, META], F32R)
        xt = sb("x_tiles", [P, NT, D])
        junk = sb("junk", [P, D])
        g1 = sb("norm1_rows", [P, D])
        msq = sb("mean_sq", [P, NT])
        ms = sb("mean_sq_eps", [P, NT])
        rstd = sb("rstd", [P, NT])
        xa = sb("xa", [P, T])
        gated = sb("gated", [P, 3, W])
        outer = sb("outer_gate", [P, 3, W])
        zp = sb("z_pool", [P, 3, W])
        meta3 = sb("meta3", [P, 3, 3, META])
        win = sb("window_sums", [P, 4, W])
        res = sb("mix_tiles", [P, 2, T])
        cw = sb("conv_w", [P, 3, 3])
        ps = sb("pool_scale", [P, 3])
        icnt = sb("inv_counts", [P, 3, HALO])
        xf_st = sb("xf_stage", [P, 2, FOUR])
        bank = ctx.enter_context(nc.psum_tensor("proj_bank", [P, 8, 512], F32))
        flat = lambda a: a.rearrange("p t n -> p (t n)")
        raw = [flat(a[:, :, :])[:, 0:D] for a in (gated, outer, zp)]
        RAW = len(raw)
        wp = [a[0:GROUP] for a in (flat(win[:, :, :])[:, 0:D], flat(win[:, :, :])[:, D:2 * D], flat(res[:, :, :]),
                                   xt[:, NT - 1, :])]
        pw = xa[0:GROUP, 0:4 * GROUP].rearrange("p (g o) -> p g o", g=4)
        z_meta = flat(win[0:META, :, :])

        consts = sem("consts_landed")
        raw_landed = [sem(f"raw_landed{i}") for i in range(RAW)]
        wp_landed = sem("wp_landed")
        w_hi_done, w_lo_done = sem("w_in_hi_made"), sem("w_in_lo_made")
        fold_done, fold_hi, fold_lo = sem("fold_done"), sem("fold_hi"), sem("fold_lo")
        z_meta_done, z_meta_read = sem("z_meta_done"), sem("z_meta_read")
        landed = [sem(f"x_landed{i}") for i in range(NT)]
        squared, rstd_made, rstd_step, normed = sem("squared"), sem("rstd_made"), sem("rstd_step"), sem("normed")
        transposed, u_hi_made, u_lo_made = sem("transposed"), sem("u_hi_made"), sem("u_lo_made")
        panel_done, read_act, gated_made = sem("panel_done"), sem("read_act"), sem("gated_made")
        carried, step = sem("carried"), sem("vector_step")
        mix_made = sem("mix_made")
        mix_stored = [sem(f"mix_stored{i}") for i in range(2)]
        tail_made = sem("tail_made")
        xf_done, xf_read = sem("xf_done"), sem("xf_read")
        xf_stored = [sem(f"xf_stored{i}") for i in range(2)]
        block = ctx.enter_context(nc.Block())

        PLAIN = [j for j in range(NPAN)] + [NPAN + 3, NPAN + 4]
        META_GROUPS = [(0, 4), (4, 4), (8, 4), (NPAN + 3, 2)]
        XA, GC, GB, ZP = range(4)
        ORDER = [q for t in range(3) for q in (t, 6 + t, 3 + t, NPAN + t)]
        READ = {XA: 1, GB: 2, ZP: 3}

        def folded(w, g, h):
            return w[:, NPAN:NPAN + 3, 4 * h:4 * h + 4, 32 * g:32 * g + 32]

        def fold_bank(n):
            return bank[:, n % 4, 0:4 * GROUP].rearrange("p (k t j) -> p t k j", k=4, t=3)

        def panel_view(a):
            return a.rearrange("p (k n) -> p k n", k=KD)

        def tile(r, t):
            return 4 * r - 3 + t

        def rounds(eng, body, flush=None):
            with eng.Fori(1, NB1 + 1) as r:
                body(r, True)
            if flush:
                flush(0)
            body(NB1 + 1, False)
            if flush:
                flush(1)

        @block.sync
        def _(sp):
            sp.dma_start(xt[0:META, 0, :], c["meta"]).then_inc(landed[0], 16)
            for dst, name in ((g1[:, :], "norm1_rows"), (half[:, :], "minus_half"), (eps[:, :], "eps"),
                              (ident[:, :], "ident"), (cw[:, :, :], "conv_cols"), (ps[:, :], "pool_scale_cols"),
                              (icnt[:, :, :], "inv_counts")):
                sp.dma_start(dst, c[name]).then_inc(consts, 16)
            for s in (*mix_stored, *xf_stored):
                sp.nop().then_inc(s, 16)

            def load(r, t):
                row = T * r + P * t
                sp.dma_start(xt[:, t, :], c["x"][bass.ds(row, P), :]).then_inc(landed[t], 16)

            sp.dma_start(pw, c["pool_w"].rearrange("g j o -> j g o")).then_inc(wp_landed, 16)
            for g in range(4):
                sp.dma_start(wp[g], c["w_pool_T"][g, :, :]).then_inc(wp_landed, 16)
            for n in range(len(PLAIN)):
                if n >= RAW:
                    sp.wait_ge(w_lo_done, n - RAW + 1)
                sp.dma_start(raw[n % RAW], c["w_in_panels"][n, :, :]).then_inc(raw_landed[n % RAW], 16)
                if n == 4:
                    for t in (1, 0, 2):
                        if t == 0:
                            sp.wait_ge(transposed, 2)
                        load(0, t)
                if n == 6:
                    sp.wait_ge(fold_done, 8)
                    load(0, NT - 1)

            sp.wait_ge(xf_read, 2)
            for row in (0, L1):
                sp.dma_start(c["xf"][row:row + META, :], xf_st[0:META, 1, :]).then_inc(xf_stored[1], 16)

            def body(r, more):
                if more:
                    for t in range(NT):
                        sp.wait_ge(transposed, 2 * tile(r, t) + 2)
                        load(r, t)
                col, skip = (T * r - T + HALO, 0) if more else (META + SEQ, HALO)
                for i in range(6):
                    row = P * (i // 2 + 3 * (i % 2))
                    sp.wait_ge(mix_made, 6 * r - 6 + i + 1)
                    sp.dma_start(c["mixT"][row:row + P, bass.ds(col, T - skip)], res[:, i % 2, skip:T])\
                        .then_inc(mix_stored[i % 2], 16)
                for t in range(NT):
                    sp.wait_ge(xf_read, tile(r, t) + 2)
                    row = T * r - T + META + P * t if more else L1 + META + P * t
                    sp.dma_start(c["xf"][bass.ds(row, P), :], xf_st[:, t % 2, :]).then_inc(xf_stored[t % 2], 16)

            def flush(q):
                sp.wait_ge(tail_made, q + 1)
                col = META + (SEQ, SEQ + DEC)[q] - HALO
                sp.dma_start(c["mixT"][0:6 * P, col:col + HALO].rearrange("(i p) n -> p i n", p=P),
                             tail[:, :, :]).then_inc(tail_stored, 16)

            rounds(sp, body, flush)
            for s in mix_stored:
                sp.wait_ge(s, 16 * (1 + 3 * NBLK))
            sp.wait_ge(xf_stored[0], 16 * (1 + 2 * NBLK))
            sp.wait_ge(xf_stored[1], 16 * (3 + 2 * NBLK))

        @block.gpsimd
        def _(pool):
            pool.wait_ge(consts, 16 * 7)

            def rms(n, rows, t):
                pool.wait_ge(squared, n + 1)
                pool.tensor_tensor(ms[0:rows, t:t + 1], msq[0:rows, t:t + 1], eps[0:rows, :], ALU.add)\
                    .then_inc(rstd_step, 1)
                pool.wait_ge(rstd_step, n + 1)
                pool.tensor_tensor(rstd[0:rows, t:t + 1], ms[0:rows, t:t + 1], half[0:rows, 0:1], ALU.pow)\
                    .then_inc(rstd_made, 1)

            rms(0, META, 0)
            with pool.Fori(1, NBLK + 1) as r:
                for t in range(NT):
                    rms(tile(r, t), P, t)

        @block.scalar
        def _(act):
            act.nop().then_inc(xf_read, 1)

            def square(r, t, rows=P):
                act.wait_ge(landed[t], 16 * (r + (t == 0)))
                if not isinstance(r, int) or r:
                    act.wait_ge(squared, tile(r, t))
                act.activation(junk[0:rows, :], xt[0:rows, t, :], ACT.Square, scale=D ** -0.5,
                               accum_out=msq[0:rows, t:t + 1]).then_inc(squared, 1)

            def u_split(n, dst, rows=P):
                for h in range(2):
                    act.wait_ge(transposed, 2 * n + h + 1)
                    act.activation(dst(h), bank[:, 6 + h, :].rearrange("p (k n) -> p k n", k=4)[:, :, 0:rows],
                                   ACT.Copy).then_inc(u_hi_made, 1)

            def u_tile(r, t):
                u_split(tile(r, t), lambda h: u_hi[:, 4 * h:4 * h + 4, P * t:P * t + P])

            def w_split(n):
                act.wait_ge(raw_landed[n % RAW], 16 * (n // RAW + 1))
                act.activation(w_hi[:, PLAIN[n], :, :], panel_view(raw[n % RAW]), ACT.Copy).then_inc(w_hi_done, 1)

            def fold_split(n):
                act.wait_ge(fold_done, n + 1)
                for t in range(3):
                    ins = act.activation(folded(w_hi, n // 2, n % 2)[:, t], fold_bank(n)[:, t], ACT.Copy)
                ins.then_inc(fold_hi, 1)

            def z_meta_read_out(i):
                j, n = META_GROUPS[i]
                act.wait_ge(z_meta_done, i + 1)
                act.activation(z_meta[:, P * j:P * (j + n)], bank[0:META, 4 + i % 2, 0:P * n], ACT.Copy)\
                    .then_inc(z_meta_read, 1)

            square(0, 0, META)
            u_split(0, lambda h: um_hi[:, 4 * h:4 * h + 4, :], META)
            for n in range(4):
                w_split(n)
            for n in range(8):
                fold_split(n)
            for n in range(4, 8):
                w_split(n)
            z_meta_read_out(0)
            square(1, 0)
            square(1, 1)
            w_split(8)
            z_meta_read_out(1)
            u_tile(1, 0)
            for n in (9, 10):
                w_split(n)
            square(1, 2)
            square(1, 3)
            z_meta_read_out(2)
            u_tile(1, 1)
            act.wait_ge(xf_done, 1)
            act.activation(xf_st[0:META, 1, :], bank[0:META, 5, 0:FOUR], ACT.Copy).then_inc(xf_read, 1)
            u_tile(1, 2)
            u_tile(1, 3)
            act.wait_ge(panel_done, 12)
            part = lambda i: bank[:, 0, 3 * META * i:3 * META * (i + 1)]
            act.activation(xa[:, 0:3 * META], part(0), ACT.Copy).then_inc(read_act, 1)
            for dst, i in ((meta3[:, 1, :, :], 1), (outer[:, :, 0:META], 1), (meta3[:, 2, :, :], 3),
                           (zp[:, :, 0:META], 3)):
                act.activation(dst, part(i).rearrange("p (t n) -> p t n", t=3), ACT.Copy).then_inc(read_act, 2)

            def body(r, more):
                for i in range(12):
                    t, q = i // 4, i % 4
                    if q == GC:
                        continue
                    act.wait_ge(panel_done, 12 * r + i + 1)
                    if q == XA:
                        dst = xa[:, 0:T]
                        act.wait_ge(gated_made, 3 * r + t)
                    elif q == GB:
                        dst = outer[:, t, META:W]
                        act.wait_ge(carried, 6 * r - 6 + 2 * t + 1)
                    else:
                        dst = zp[:, t, META:W]
                        act.wait_ge(carried, 6 * r - 6 + 2 * t + 2)
                    if not more and i == GB:
                        act.wait_ge(tail_made, 1)
                    act.activation(dst, bank[:, q, :], ACT.Copy).then_inc(read_act, 1)
                    if more and i in (2, 4, 6, 8):
                        square(r + 1, i // 2 - 1)
                for t in range(NT):
                    s = t % 2
                    act.wait_ge(xf_done, tile(r, t) + 1)
                    act.wait_ge(xf_stored[s], 16 * (2 * r - 2 + t // 2 + 1 + 2 * s))
                    act.activation(xf_st[:, s, :], bank[:, 4 + s, 0:FOUR], ACT.Copy).then_inc(xf_read, 1)
                    if more:
                        u_tile(r + 1, t)

            rounds(act, body)

        @block.vector
        def _(dve):
            dve.wait_ge(consts, 16 * 7)
            STEPS = 3 * 3 + 3 * 8
            CONV_TAIL_STEPS = 2 + 3 * 4
            TAIL_STEPS = CONV_TAIL_STEPS + 1 + 4 + 4 + 1 + 3 + 3

            def norm(n, t, rows=P):
                dve.wait_ge(rstd_made, n + 1)
                dve.scalar_tensor_tensor(out=xt[0:rows, t, :], in0=xt[0:rows, t, :], scalar=rstd[0:rows, t:t + 1],
                                         in1=g1[0:rows, :], op0=ALU.mult, op1=ALU.mult).then_inc(normed, 1)

            def u_split(n, hi, lo, rows=P):
                for h in range(2):
                    dve.wait_ge(u_hi_made, 2 * n + h + 1)
                    dve.tensor_tensor(lo(h), bank[:, 6 + h, :].rearrange("p (k n) -> p k n", k=4)[:, :, 0:rows],
                                      hi(h).bitcast(F32), ALU.subtract).then_inc(u_lo_made, 1)

            def u_tile(r, t):
                part = lambda u: lambda h: u[:, 4 * h:4 * h + 4, P * t:P * t + P]
                u_split(tile(r, t), part(u_hi), part(u_lo))

            def w_split(n):
                dve.wait_ge(w_hi_done, n + 1)
                dve.tensor_tensor(w_lo[:, PLAIN[n], :, :], panel_view(raw[n % RAW]),
                                  w_hi[:, PLAIN[n], :, :].bitcast(F32), ALU.subtract).then_inc(w_lo_done, 1)

            def fold_split(n):
                dve.wait_ge(fold_hi, n + 1)
                for t in range(3):
                    ins = dve.tensor_tensor(folded(w_lo, n // 2, n % 2)[:, t], fold_bank(n)[:, t],
                                            folded(w_hi, n // 2, n % 2)[:, t].bitcast(F32), ALU.subtract)
                ins.then_inc(fold_lo, 1)

            norm(0, 0, META)
            part = lambda u: lambda h: u[:, 4 * h:4 * h + 4, :]
            u_split(0, part(um_hi), part(um_lo), META)
            for n in range(4):
                w_split(n)
            for n in range(8):
                fold_split(n)
            for n in range(4, 8):
                w_split(n)
            norm(tile(1, 0), 0)
            norm(tile(1, 1), 1)
            w_split(8)
            u_tile(1, 0)
            for n in (9, 10):
                w_split(n)
            norm(tile(1, 2), 2)
            norm(tile(1, 3), 3)
            u_tile(1, 1)
            u_tile(1, 2)
            u_tile(1, 3)
            gc = bank[:, 0, 6 * META:9 * META].rearrange("p (t n) -> p t n", t=3)
            xa_meta = xa[:, 0:3 * META].rearrange("p (t n) -> p t n", t=3)
            dve.wait_ge(read_act, 9)
            dve.tensor_tensor(meta3[:, 0, :, :], gc, xa_meta, ALU.mult).then_inc(gated_made, 1)
            dve.tensor_tensor(gated[:, :, 0:META], gc, xa_meta, ALU.mult).then_inc(gated_made, 2)
            dve.wait_ge(gated_made, 3)
            dve.engine_nop().then_inc(carried, 6)

            def conv(ch, t, dst, n, out_sem):
                g = lambda d: gated[:, t, HALO + d:HALO + d + n]
                ch.step(dve.tensor_scalar(dst, g(-1), cw[:, t, 0:1], None, ALU.mult))
                for d in (0, 1):
                    ch.step(dve.scalar_tensor_tensor(out=dst, in0=g(d), scalar=cw[:, t, d + 1:d + 2], in1=dst,
                                                     op0=ALU.mult, op1=ALU.add))
                ins = dve.tensor_tensor(dst, dst, outer[:, t, HALO:HALO + n], ALU.mult)
                ins.then_inc(out_sem, 1)
                return ins

            def windows(ch, t, n):
                m = n + META - 1
                src, d = zp[:, t, :], 1
                for g in range(4):
                    ch.step(dve.tensor_tensor(win[:, g, 0:m], src[:, 0:m], src[:, d:d + m], ALU.add))
                    src, d = win[:, g, :], 2 * d
                    m -= d

            def body(r, more):
                ch = Chain(dve, step, STEPS * (r - 1) + (0 if more else TAIL_STEPS))
                for t in range(3):
                    dve.wait_ge(panel_done, 12 * r + 4 * t + GC + 1)
                    dve.wait_ge(read_act, 9 * r + 3 * t + READ[XA])
                    dve.tensor_tensor(gated[:, t, META:W], bank[:, GC, :], xa[:, 0:T], ALU.mult)\
                        .then_inc(gated_made, 1)
                    dve.wait_ge(gated_made, 3 * r + t + 1)
                    dve.wait_ge(carried, 6 * r - 6 + 2 * t + 1)
                    dve.wait_ge(read_act, 9 * r + 3 * t + READ[GB])
                    dve.wait_ge(mix_stored[0], 16 * (3 * r - 3 + t + 1))
                    conv(ch, t, res[:, 0, :], T, mix_made)
                    dve.wait_ge(mix_made, 6 * r - 6 + 2 * t + 1)
                    dve.tensor_copy(gated[:, t, 0:META], gated[:, t, T:W])
                    dve.tensor_copy(outer[:, t, 0:META], outer[:, t, T:W]).then_inc(carried, 1)
                    if more and t:
                        norm(tile(r + 1, 2 * t - 1), 2 * t - 1)
                    if not more and t == 2:
                        dve.wait_ge(carried, 6 * r + 2 * t + 1)
                        dve.wait_ge(tail_stored, 16)
                        flush_conv(ch)
                    dve.wait_ge(read_act, 9 * r + 3 * t + READ[ZP])
                    dve.wait_ge(carried, 6 * r - 6 + 2 * t + 2)
                    windows(ch, t, T)
                    if more and t == 2:
                        u_tile(r + 1, 0)
                    dve.wait_ge(mix_stored[1], 16 * (3 * r - 3 + t + 1))
                    for g, w in enumerate(WINDOWS):
                        q = slice(32 * g, 32 * g + 32)
                        ch.step(dve.scalar_tensor_tensor(
                            out=res[q, 1, :], in0=win[q, g, HALO - w // 2:HALO - w // 2 + T], scalar=1.0 / w,
                            in1=zp[q, t, HALO:HALO + T], op0=ALU.mult, op1=ALU.subtract))
                    dve.tensor_scalar(res[:, 1, :], res[:, 1, :], ps[:, t:t + 1], None, ALU.mult)\
                        .then_inc(mix_made, 1)
                    dve.wait_ge(mix_made, 6 * r - 6 + 2 * t + 2)
                    dve.tensor_copy(zp[:, t, 0:META], zp[:, t, T:W]).then_inc(carried, 1)
                    if more and t < 2:
                        norm(tile(r + 1, 2 * t), 2 * t)
                if more:
                    for t in range(1, NT):
                        u_tile(r + 1, t)
                assert ch.n == STEPS + (0 if more else CONV_TAIL_STEPS)

            def flush_conv(ch):
                for buf in (gated, outer):
                    ch.step(dve.memset(buf[:, :, META:META + HALO], 0.0))
                for t in range(3):
                    ch.step(conv_tail(ch, t))

            def flush(q):
                base = STEPS * NB1 if q == 0 else STEPS * NBLK + TAIL_STEPS + CONV_TAIL_STEPS
                ch = Chain(dve, step, base)
                dve.wait_ge(carried, 6 * (1 + (NB1 if q == 0 else NBLK)))
                if q == 0:
                    flush_conv(ch)
                ch.step(dve.memset(zp[:, :, META:META + HALO], 0.0))
                sums = [win[:, g, 0:3 * (META + HALO)].rearrange("p (t n) -> p t n", t=3) for g in range(4)]
                src, d, m = zp, 1, META + HALO - 1
                for g in range(4):
                    ch.step(dve.tensor_tensor(sums[g][:, :, 0:m], src[:, :, 0:m], src[:, :, d:d + m], ALU.add))
                    src, d = sums[g], 2 * d
                    m -= d
                for g, w in enumerate(WINDOWS):
                    s = slice(32 * g, 32 * g + 32)
                    ch.step(dve.tensor_tensor(tail[s, 3:6, :], sums[g][s, :, HALO - w // 2:2 * HALO - w // 2],
                                              icnt[s, :, :], ALU.mult))
                ch.step(dve.tensor_tensor(tail[:, 3:6, :], tail[:, 3:6, :], zp[:, :, HALO:2 * HALO], ALU.subtract))
                for t in range(3):
                    ch.step(dve.tensor_scalar(tail[:, 3 + t, :], tail[:, 3 + t, :], ps[:, t:t + 1], None, ALU.mult))
                if q == 0:
                    for b, buf in enumerate((gated, outer, zp)):
                        ch.step(dve.tensor_copy(buf[:, :, 0:META], meta3[:, b, :, :]))
                assert ch.n == TAIL_STEPS - (3 + CONV_TAIL_STEPS) * q
                dve.engine_nop().then_inc(tail_made, 1)

            def conv_tail(ch, t):
                dst = tail[:, t, :]
                g = lambda d: gated[:, t, HALO + d:2 * HALO + d]
                ch.step(dve.tensor_scalar(dst, g(-1), cw[:, t, 0:1], None, ALU.mult))
                for d in (0, 1):
                    ch.step(dve.scalar_tensor_tensor(out=dst, in0=g(d), scalar=cw[:, t, d + 1:d + 2], in1=dst,
                                                     op0=ALU.mult, op1=ALU.add))
                return dve.tensor_tensor(dst, dst, outer[:, t, HALO:2 * HALO], ALU.mult)

            rounds(dve, body, flush)

        @block.tensor
        def _(pe):
            pe.wait_ge(consts, 16 * 7)

            def transpose(n, t, rows=P):
                pe.wait_ge(normed, n + 1)
                for h in range(2):
                    if not isinstance(n, int) or n:
                        pe.wait_ge(u_lo_made, 2 * n + h - 1)
                    for k in range(4):
                        ins = pe.transpose(bank[:, 6 + h, P * k:P * k + rows],
                                           xt[0:rows, t, (4 * h + k) * P:(4 * h + k + 1) * P],
                                           ident[0:rows, 0:rows])
                    ins.then_inc(transposed, 1)

            transpose(0, 0, META)
            pe.wait_ge(wp_landed, 16 * 5)
            for n in range(8):
                g, h = n // 2, n % 2
                if n >= 4:
                    pe.wait_ge(fold_lo, n - 3)
                for k in range(4):
                    ins = pe.matmul(bank[:, n % 4, k * GROUP:(k + 1) * GROUP],
                                    wp[g][:, (4 * h + k) * P:(4 * h + k + 1) * P], pw[:, g, :],
                                    start=True, stop=True)
                ins.then_inc(fold_done, 1)
            pe.wait_ge(u_lo_made, 2)
            for i, (j, n) in enumerate(META_GROUPS):
                pe.wait_ge(w_lo_done, (4, 8, 9, 11)[i])
                if i == 2:
                    pe.wait_ge(fold_lo, 8)
                if i >= 2:
                    pe.wait_ge(z_meta_read, i - 1)
                for k in range(KD):
                    ins = split_product(pe, bank[0:META, 4 + i % 2, 0:P * n].rearrange("p (a n) -> p a n", a=n),
                                        (um_hi[:, k, :], um_lo[:, k, :]),
                                        [w[:, j:j + n, k, :] for w in (w_hi, w_lo)], k == 0, k == KD - 1)
                ins.then_inc(z_meta_done if i < 3 else xf_done, 1)
                if i:
                    transpose(tile(1, i - 1), i - 1)
            transpose(tile(1, NT - 1), NT - 1)
            pe.wait_ge(z_meta_read, 3)
            for j in range(NPAN + 3):
                ins = pe.transpose(bank[:, 0, META * j:META * (j + 1)], z_meta[:, P * j:P * (j + 1)],
                                   ident[0:META, 0:META])
            ins.then_inc(panel_done, 12)

            def body(r, more):
                pe.wait_ge(u_lo_made, 2 * tile(r, NT - 1) + 2)
                for i, j in enumerate(ORDER):
                    t, q = i // 4, i % 4
                    if q == GC:
                        pe.wait_ge(gated_made, 3 * r + t)
                    else:
                        pe.wait_ge(read_act, 9 * r + 3 * t - 3 + READ[q])
                    if i == 0:
                        pe.wait_ge(gated_made, 3 * r)
                    for k in range(KD):
                        ins = split_product(pe, bank[:, q, :], (w_hi[:, j, k, :], w_lo[:, j, k, :]),
                                            (u_hi[:, k, :], u_lo[:, k, :]), k == 0, k == KD - 1)
                    ins.then_inc(panel_done, 1)
                for t in range(NT):
                    pe.wait_ge(xf_read, tile(r, t))
                    tk = slice(P * t, P * t + P)
                    for k in range(KD):
                        wf = [w[:, NPAN + 3:NPAN + 5, k, :] for w in (w_hi, w_lo)]
                        ins = split_product(pe, bank[:, 4 + t % 2, 0:FOUR].rearrange("p (a n) -> p a n", a=2),
                                            (u_hi[:, k, tk], u_lo[:, k, tk]), wf, k == 0, k == KD - 1)
                    ins.then_inc(xf_done, 1)
                    if more:
                        transpose(tile(r + 1, t), t)

            rounds(pe, body)


def first_token(b):
    return T * (0 - b) + T * (NBLK - 1)


class Feed:

    def __init__(self, nc, ctx, c):
        sb = lambda n, s, d=F32: ctx.enter_context(nc.sbuf_tensor(n + "_sb", s, d))
        sem = lambda n: ctx.enter_context(nc.semaphore(n))
        self.c = c
        self.w_raw = sb("w_raw", [P, RING, D])
        self.w_hi = sb("w_panel_hi", [P, RING, D], F32R)
        self.w_lo = sb("w_panel_lo", [P, RING, D], F32R)
        self.v_hi = sb("v_hi", [P, KD, T], F32R)
        self.v_lo = sb("v_lo", [P, KD, T], F32R)
        self.mx = sb("mix_raw", [P, 2, T])
        self.mix_g = sb("mix_g_cols", [P, KD])
        self.squares = sb("mix_squares", [P, 3, T])
        self.group_means = sb("group_means", [P, 3])
        self.g_landed = sem("mix_g_landed")
        self.w_landed = [sem(f"w_landed{i}") for i in range(RING)]
        self.w_hi_made, self.w_lo_made, self.w_used = sem("w_hi_made"), sem("w_lo_made"), sem("w_used")
        self.m_landed = [sem(f"mix_landed{i}") for i in range(2)]
        self.m_hi_made, self.m_lo_made = sem("m_hi_made"), sem("m_lo_made")
        self.squares_step, self.m_used = sem("squares_step"), sem("m_used")
        self.f_stored, self.f_last_stored = sem("f_stored"), sem("f_last_stored")
        self.first_raw = None
        self.first_landed = [sem(f"first_mix_landed{k}") for k in range(KD)]

    def raw_mix(self, b, k):
        return self.first_raw[k] if isinstance(b, int) and b == 0 else self.mx[:, k % 2, :]

    def freed(self, b, q):
        if not isinstance(q, int) or q >= RING:
            return PER * b + q + 1
        return PER * b + max(j for j in range(PER) if j % RING == q) - PER + 1 + RING

    def load_mix(self, sp, b, k):
        src = self.c["mixT"][P * k:P * k + P, bass.ds(first_token(b) + META, T)]
        if isinstance(b, int) and b == 0:
            sp.dma_start(self.raw_mix(b, k), src).then_inc(self.first_landed[k], 16)
        else:
            sp.wait_ge(self.m_used, KD * b + k + 1)
            sp.dma_start(self.raw_mix(b, k), src).then_inc(self.m_landed[k % 2], 16)

    def split_mix_hi(self, act, b, k):
        if isinstance(b, int) and b == 0:
            act.wait_ge(self.first_landed[k], 16)
        else:
            act.wait_ge(self.m_landed[k % 2], 16 * (KD // 2 * (b - 1) + k // 2 + 1))
        act.activation(self.v_hi[:, k, :], self.raw_mix(b, k), ACT.Copy, scale=self.mix_g[:, k:k + 1])\
            .then_inc(self.m_hi_made, 1)

    def split_mix_lo(self, dve, b, k):
        dve.wait_ge(self.m_hi_made, KD * b + k + 1)
        dve.scalar_tensor_tensor(out=self.v_lo[:, k, :], in0=self.raw_mix(b, k), scalar=self.mix_g[:, k:k + 1],
                                 in1=self.v_hi[:, k, :].bitcast(F32), op0=ALU.mult, op1=ALU.subtract)\
            .then_inc(self.m_lo_made, 1)

    def square_mix(self, pool, b, k):
        g, raw = GROUP_OF[k], self.raw_mix(b, k)
        pool.wait_ge(self.m_lo_made, KD * b + k + 3)
        if k in FIRST:
            pool.tensor_tensor(self.squares[:, g, :], raw, raw, ALU.mult).then_inc(self.m_used, 1)
        else:
            pool.tensor_tensor(raw, raw, raw, ALU.mult).then_inc(self.squares_step, 1)
            pool.wait_ge(self.squares_step, (KD - 3) * b + k - g)
            pool.wait_ge(self.m_used, KD * b + k + 2)
            pool.tensor_tensor(self.squares[:, g, :], self.squares[:, g, :], raw, ALU.add)\
                .then_inc(self.m_used, 1)

    def load_panel(self, sp, b, q, s):
        past = PER * b + START.index(q - RING) + 1 + RING if isinstance(q, int) and RING <= q < 2 * RING \
            else self.freed(b, q)
        sp.wait_ge(self.w_lo_made, past)
        sp.dma_start(self.w_raw[:, s, :], self.c["w_panels"][bass.ds(q, 1), :, :].rearrange("a p n -> p (a n)"))\
            .then_inc(self.w_landed[s], 16)

    def split_panel_hi(self, act, b, q, s, turn=None):
        act.wait_ge(self.w_landed[s], 16 * (USES[s] * b + (q // RING + 1 if turn is None else turn + 1)))
        act.wait_ge(self.w_used, self.freed(b, q))
        act.activation(self.w_hi[:, s, :], self.w_raw[:, s, :], ACT.Copy).then_inc(self.w_hi_made, 1)

    def split_panel_lo(self, dve, b, q, s):
        place = START.index(q) if isinstance(q, int) and q < RING else q
        dve.wait_ge(self.w_hi_made, PER * b + place + 1)
        dve.tensor_tensor(self.w_lo[:, s, :], self.w_raw[:, s, :], self.w_hi[:, s, :].bitcast(F32), ALU.subtract)\
            .then_inc(self.w_lo_made, 1)


def fourier(nc, c, feed, tail_stored):
    EXTRA = L1 // 2 % P + 1
    TILES1, TILES2 = L1 // 2 // P + 1, L2 // 2 // P + 1
    TILES, PIECE = TILES1 + TILES2, 3
    assert L2 // 2 % P + 1 == EXTRA and TILES2 == PIECE and TILES1 % PIECE == 0
    SLOTS = 3
    CH = KCH
    with ExitStack() as ctx:
        sb = lambda n, s, d=F32: ctx.enter_context(nc.sbuf_tensor(n + "_sb", s, d))
        sem = lambda n: ctx.enter_context(nc.semaphore(n))
        xf = sb("xf", [P, TILES, FOUR])
        x_hi = sb("xf_folded_hi", [P, 2, TILES, FOUR], F32R)
        x_lo = sb("xf_folded_lo", [P, 2, TILES, FOUR], F32R)
        heads = sb("head_tables", [P, 2, P])
        b_hi = sb("head_hi", [P, 2, P], F32R)
        b_lo = sb("head_lo", [P, 2, P], F32R)
        raw = sb("table_raw", [P, SLOTS, 2, CH])
        t_hi = sb("table_hi", [P, SLOTS, 2, CH], F32R)
        t_lo = sb("table_lo", [P, SLOTS, 2, CH], F32R)
        pq_hi = sb("pq_hi", [P, 4, CH], F32R)
        pq_lo = sb("pq_lo", [P, 4, CH], F32R)
        odd = sb("odd_part", [P, 2, CH])
        fwd = sb("f_forward", [P, 2, CH])
        rev = sb("f_reversed", [P, 2, CH])
        bank = ctx.enter_context(nc.psum_tensor("dft_bank", [P, 8, 512], F32))
        reversal = sb("reversal", [P, P])
        partner = feed.w_raw.rearrange("p s (a n) -> p (s a) n", n=FOUR)[:, 0:TILES, :]
        diff = [feed.squares.rearrange("p g (a n) -> p (g a) n", n=FOUR)[:, i:i + PIECE, :] for i in (0, PIECE)]

        S1, S2 = list(range(TILES2, TILES)), list(range(TILES2))
        PER1, PER2 = len(S1), len(S2)
        assert PER1 % SLOTS == PER2 % SLOTS
        PIECES = TILES // PIECE

        xf_landed, heads_landed = [sem(f"xf_landed{i}") for i in range(PIECES)], sem("heads_landed")
        reversal_landed = sem("reversal_landed")
        cleared, turned, folded_made = sem("cleared"), sem("turned"), sem("folded_made")

        def turn_tiles(q):
            return bank[:, 4 + 2 * (q % 2):6 + 2 * (q % 2), :].rearrange("p b (a n) -> p (b a) n", n=FOUR)[:, 0:PIECE, :]

        t_landed = [sem(f"t_landed{i}") for i in range(SLOTS)]
        xf_hi_made, xf_lo_made = sem("xf_hi_made"), sem("xf_lo_made")
        b_hi_made, b_lo_made = sem("b_hi_made"), sem("b_lo_made")
        t_hi_made, t_lo_made, t_used = sem("t_hi_made"), sem("t_lo_made"), sem("t_used")
        pq_hi_made, pq_lo_made = sem("pq_hi_made"), sem("pq_lo_made")
        head_done, odd_made, f_made = sem("head_done"), sem("odd_made"), sem("f_made")
        f_stored = feed.f_stored
        xf_rows = xf.rearrange("p (k a) n -> p k (a n)", a=T // FOUR)
        feed.first_raw = [xf_rows[:, k, :] for k in range(TILES * FOUR // T)]
        feed.first_raw += [feed.mx[:, k % 2, :] for k in range(len(feed.first_raw), KD)]
        assert len(feed.first_raw) == KD
        block = ctx.enter_context(nc.Block())

        def before(ch):
            return PER1 * ch + (PER2 - PER1 if not isinstance(ch, int) or ch else 0)

        def freed(ch, i):
            if i >= SLOTS:
                return before(ch) + i + 1
            return before(ch) + max(j for j in range(PER1) if j % SLOTS == i) - PER1 + 1 + SLOTS

        def turn(ch, i):
            s = i % SLOTS
            uses1, uses2 = len(range(s, PER1, SLOTS)), len(range(s, PER2, SLOTS))
            return i // SLOTS + 1 + (uses1 * (ch - 1) + uses2 if not isinstance(ch, int) or ch else 0)

        def chunks(step, chunk_end, eng, after=None):
            for i, ti in enumerate(S2):
                step(0, i, ti, K2)
                if after:
                    after(0, i)
            chunk_end(0, K2)
            with eng.Fori(1, NCH) as ch:
                for i, ti in enumerate(S1[HEAD:]):
                    step(ch, i + HEAD, ti, CH)
                chunk_end(ch, CH)
            for i, ti in enumerate(S1[HEAD:]):
                step(NCH, i + HEAD, ti, CH)
                if after:
                    after(NCH, i)
            chunk_end(NCH, CH)

        HEAD = 3
        is_last = lambda ch: isinstance(ch, int) and ch == NCH
        STARTERS = [("panel", q) for q in START] + [("mix", k) for k in range(KD)]
        assert len(STARTERS) <= 2 * (PER1 - HEAD)

        def rows_of(ti):
            return EXTRA if ti in (TILES2 - 1, TILES - 1) else P

        def stores(ch, n):
            first = isinstance(ch, int) and ch == 0
            middle = int(first or is_last(ch))
            skip = META - 1 if first else 0
            k0, r0 = (SEQ + META, SEQ + L2 - n) if first else (CH * (ch - 1) + 1, CH * (0 - ch) + L1)
            dst = c["mixT"][2 * CONV:D, :].rearrange("(m p) n -> p m n", p=P)
            return ((dst[:, :, bass.ds(r0 + middle, n - middle)], rev[:, :, middle:n]),
                    (dst[:, :, bass.ds(k0, n - skip)], fwd[:, :, skip:n]))

        @block.sync
        def _(sp):
            def piece(q):
                base, length = (L1, L2) if q == 0 else (0, L1)
                n0 = 1 + PIECE * P * max(q - 1, 0)
                full = PIECE - 1 if q in (0, PIECES - 1) else PIECE
                rows = full * P
                tiles = slice(PIECE * q, PIECE * q + full)
                there = c["xf"][base + n0:base + n0 + rows, :]
                sp.dma_start(xf[:, tiles, :], there.rearrange("(t p) n -> p t n", p=P)).then_inc(xf_landed[q], 16)
                for i in range(full):
                    end = base + length - n0 + 1 - P * i
                    sp.dma_start(partner[:, PIECE * q + i, :], c["xf"][end - P:end, :]).then_inc(xf_landed[q], 16)
                if full < PIECE:
                    last, n1 = PIECE * q + full, n0 + rows
                    sp.wait_ge(cleared, 4)
                    sp.dma_start(xf[0:EXTRA - 1, last, :], c["xf"][base + n1:base + n1 + EXTRA - 1, :])\
                        .then_inc(xf_landed[q], 16)
                    sp.dma_start(xf[EXTRA - 1:EXTRA, last, :], c["xf"][base:base + 1, :]).then_inc(xf_landed[q], 16)
                    end = base + length - n1 + 1
                    sp.dma_start(partner[P - EXTRA + 2:P, last, :], c["xf"][end - EXTRA + 2:end, :])\
                        .then_inc(xf_landed[q], 16)

            def step(ch, i, ti, n):
                sp.wait_ge(t_lo_made, freed(ch, i))
                r = rows_of(ti)
                if n == CH:
                    src = c["table1"][bass.ds(ch - 1, 1), i, 0:r, :].rearrange("a p n -> p (a n)")
                    dst = raw[0:r, i % SLOTS, :, :].rearrange("p a n -> p (a n)")
                else:
                    src = c["table2"][i, 0:r, :].rearrange("p (a n) -> p a n", a=2)
                    dst = raw[0:r, i % SLOTS, :, 0:n]
                sp.dma_start(dst, src).then_inc(t_landed[i % SLOTS], 16)

            def chunk_end(ch, n):
                if not is_last(ch):
                    for i in range(HEAD):
                        step(ch + 1, i, S1[i], CH)
                if isinstance(ch, int) and ch == 0:
                    sp.wait_ge(turned, PIECES)
                    for q in START:
                        feed.load_panel(sp, 0, q, q)
                    sp.wait_ge(xf_lo_made, 2 * PIECES)

            def after(ch, i):
                if ch == 0:
                    piece(1 + i)
                    if i == 2:
                        sp.dma_start(heads[:, :, :], c["head_tables"]).then_inc(heads_landed, 16)
                        sp.dma_start(feed.mix_g[:, :], c["mix_g_cols"]).then_inc(feed.g_landed, 16)
                        sp.dma_start(feed.group_means[:, :], c["group_means"]).then_inc(feed.g_landed, 16)
                elif i == 0:
                    sp.wait_ge(f_stored, 32)
                    sp.wait_ge(tail_stored, 32)
                    for k in range(KD):
                        feed.load_mix(sp, 0, k)

            sp.dma_start(reversal[:, :], c["reversal"]).then_inc(reversal_landed, 16)
            piece(0)
            chunks(step, chunk_end, sp, after)
            for q in START:
                feed.load_panel(sp, 0, q + RING, q)
            sp.wait_ge(f_made, 2 * NCH + 3)
            for dst, src in stores(NCH, CH):
                sp.dma_start(dst, src).then_inc(feed.f_last_stored, 16)

        @block.gpsimd
        def _(pool):
            pool.nop().then_inc(feed.m_used, 2)
            for last in (TILES2 - 1, TILES - 1):
                pool.memset(xf[:, last, :], 0.0).then_inc(cleared, 1)
                pool.memset(partner[:, last, :], 0.0).then_inc(cleared, 1)

            def store(ch, n):
                pool.wait_ge(f_made, 2 * ch + 3)
                for dst, src in stores(ch, n):
                    pool.dma_start(dst, src).then_inc(f_stored, 16)

            store(0, K2)
            with pool.Fori(1, NCH) as ch:
                store(ch, CH)
            for k in range(KD):
                feed.square_mix(pool, 0, k)

        @block.scalar
        def _(act):
            def piece(q):
                tiles = slice(PIECE * q, PIECE * q + PIECE)
                for a, src in ((1, diff[q % 2]), (0, xf[:, tiles, :])):
                    act.wait_ge(folded_made, 2 * q + 2 - a)
                    act.activation(x_hi[:, a, tiles, :], src, ACT.Copy).then_inc(xf_hi_made, 1)

            def step(ch, i, ti, n):
                s, r = i % SLOTS, rows_of(ti)
                act.wait_ge(t_landed[s], 16 * turn(ch, i))
                act.wait_ge(t_used, freed(ch, i))
                act.activation(t_hi[0:r, s, :, 0:n], raw[0:r, s, :, 0:n], ACT.Copy).then_inc(t_hi_made, 1)

            def chunk_end(ch, n):
                if not is_last(ch):
                    step(ch + 1, 0, S1[0], CH)
                act.wait_ge(t_used, before(ch + 1) + SLOTS)
                for q in range(4):
                    act.activation(pq_hi[:, q, 0:n], bank[:, q, 0:n], ACT.Copy).then_inc(pq_hi_made, 1)
                if not is_last(ch):
                    for i in range(1, HEAD):
                        step(ch + 1, i, S1[i], CH)
                if isinstance(ch, int) and ch == 0:
                    for q in range(2, PIECES):
                        piece(q)
                act.wait_ge(f_made, 2 * ch + 1)
                for m in range(2):
                    act.wait_ge(head_done, 4 * ch + 2 * m + 2)
                    act.activation(odd[:, m, 0:n], bank[:, 6 + m, 0:n], ACT.Copy).then_inc(odd_made, 1)

            def after(ch, i):
                if ch == 0:
                    if i == len(S2) - 1:
                        piece(1)
                        act.wait_ge(heads_landed, 16)
                        act.activation(b_hi[:, :, :], heads[:, :, :], ACT.Copy).then_inc(b_hi_made, 1)
                        act.wait_ge(feed.g_landed, 32)
                else:
                    for kind, k in STARTERS[2 * i:2 * i + 2]:
                        if kind == "mix":
                            feed.split_mix_hi(act, 0, k)
                        else:
                            feed.split_panel_hi(act, 0, k, k)

            piece(0)
            chunks(step, chunk_end, act, after)

        @block.vector
        def _(dve):
            dve.nop().then_inc(t_lo_made, SLOTS)
            dve.nop().then_inc(f_made, 1)
            dve.nop().then_inc(feed.w_lo_made, RING)
            dve.nop().then_inc(feed.m_lo_made, 2)

            def piece(q):
                tiles = slice(PIECE * q, PIECE * q + PIECE)
                dve.wait_ge(turned, q + 1)
                here, there = xf[:, tiles, :], turn_tiles(q)
                dve.tensor_tensor(diff[q % 2], here, there, ALU.subtract).then_inc(folded_made, 1)
                dve.tensor_tensor(here, here, there, ALU.add).then_inc(folded_made, 1)
                dve.wait_ge(folded_made, 2 * q + 2)
                for a, src in ((1, diff[q % 2]), (0, here)):
                    dve.wait_ge(xf_hi_made, 2 * q + 2 - a)
                    dve.tensor_tensor(x_lo[:, a, tiles, :], src, x_hi[:, a, tiles, :].bitcast(F32),
                                      ALU.subtract).then_inc(xf_lo_made, 1)

            def step(ch, i, ti, n):
                s, r = i % SLOTS, rows_of(ti)
                dve.wait_ge(t_hi_made, before(ch) + i + 1)
                dve.tensor_tensor(t_lo[0:r, s, :, 0:n], raw[0:r, s, :, 0:n], t_hi[0:r, s, :, 0:n].bitcast(F32),
                                  ALU.subtract).then_inc(t_lo_made, 1)

            def chunk_end(ch, n):
                if not is_last(ch):
                    step(ch + 1, 0, S1[0], CH)
                for q in range(4):
                    dve.wait_ge(pq_hi_made, 4 * ch + q + 1)
                    dve.tensor_tensor(pq_lo[:, q, 0:n], bank[:, q, 0:n], pq_hi[:, q, 0:n].bitcast(F32),
                                      ALU.subtract).then_inc(pq_lo_made, 1)
                if not is_last(ch):
                    for i in range(1, HEAD):
                        step(ch + 1, i, S1[i], CH)
                if isinstance(ch, int) and ch == 0:
                    for q in range(2, PIECES):
                        piece(q)
                if not isinstance(ch, int) or ch:
                    dve.wait_ge(f_stored, 32 * ch)
                for m in range(2):
                    dve.wait_ge(odd_made, 2 * ch + m + 1)
                    dve.tensor_tensor(rev[:, m, 0:n][:, ::-1], bank[:, 4 + m, 0:n], odd[:, m, 0:n], ALU.add)
                    dve.tensor_tensor(fwd[:, m, 0:n], bank[:, 4 + m, 0:n], odd[:, m, 0:n], ALU.subtract)\
                        .then_inc(f_made, 1)

            def after(ch, i):
                if ch == 0:
                    if i == len(S2) - 1:
                        piece(1)
                        dve.wait_ge(b_hi_made, 1)
                        dve.tensor_tensor(b_lo[:, :, :], heads[:, :, :], b_hi[:, :, :].bitcast(F32), ALU.subtract)\
                            .then_inc(b_lo_made, 1)
                        dve.wait_ge(feed.g_landed, 32)
                else:
                    for kind, k in STARTERS[2 * i:2 * i + 2]:
                        if kind == "mix":
                            feed.split_mix_lo(dve, 0, k)
                        else:
                            feed.split_panel_lo(dve, 0, k, k)

            piece(0)
            chunks(step, chunk_end, dve, after)

        @block.tensor
        def _(pe):
            pe.nop().then_inc(t_used, SLOTS)
            pe.nop().then_inc(feed.w_used, RING)

            def turn_round(q):
                pe.wait_ge(xf_landed[q], 16 * (1 + PIECE + (2 if q in (0, PIECES - 1) else 0)))
                if q >= 2:
                    pe.wait_ge(folded_made, 2 * (q - 1))
                for i in range(PIECE):
                    ins = pe.matmul(turn_tiles(q)[:, i, :], reversal[:, :],
                                    partner[:, PIECE * q + i, :], start=True, stop=True)
                ins.then_inc(turned, 1)

            pe.wait_ge(reversal_landed, 16)
            turn_round(0)
            pe.wait_ge(xf_lo_made, 2)

            def step(ch, i, ti, n):
                s, r = i % SLOTS, rows_of(ti)
                pe.wait_ge(t_lo_made, before(ch) + i + 1 + SLOTS)
                if n == CH and isinstance(ch, int) and ch == 1 and i == 0:
                    pe.wait_ge(xf_lo_made, 4)
                last = ti in (TILES2 - 1, TILES - 1)
                for m in range(2):
                    for a in range(2):
                        w = [x[0:r, a, ti, P * m:P * m + P] for x in (x_hi, x_lo)]
                        if n == CH and i == 0:
                            pe.wait_ge(pq_lo_made, 4 * (ch - 1) + 2 * m + a + 1)
                        ins = split_product(pe, bank[:, 2 * m + a, 0:n], w,
                                            [t[0:r, s, a, 0:n] for t in (t_hi, t_lo)], i == 0, last)
                ins.then_inc(t_used, 1)

            def chunk_end(ch, n):
                if not is_last(ch):
                    for i in range(HEAD - 1):
                        step(ch + 1, i, S1[i], CH)
                        if isinstance(ch, int) and ch == 0:
                            turn_round(2 + i)
                if isinstance(ch, int) and ch == 0:
                    pe.wait_ge(b_lo_made, 1)
                    pe.wait_ge(folded_made, 2 * PIECES)
                else:
                    pe.wait_ge(f_made, 2 * ch + 1)
                for m in range(2):
                    for a in range(2):
                        pe.wait_ge(pq_lo_made, 4 * ch + 2 * m + a + 1)
                        split_product(pe, bank[:, 4 + 2 * a + m, 0:n], (b_hi[:, a, :], b_lo[:, a, :]),
                                      (pq_hi[:, 2 * m + a, 0:n], pq_lo[:, 2 * m + a, 0:n]), True, True)\
                            .then_inc(head_done, 1)
                if not is_last(ch):
                    step(ch + 1, HEAD - 1, S1[HEAD - 1], CH)
                if isinstance(ch, int) and ch == 0:
                    pe.wait_ge(xf_lo_made, 2 * PIECES)

            chunks(step, chunk_end, pe, lambda ch, i: turn_round(1) if ch == 0 and i == 0 else None)


def finish(nc, c, feed, ident, half, eps):
    BANKS = (4, 5, 6, 7, 0, 1, 2, 3)
    FIRST_TURN = (*range(1, 8), 0)
    MIX_STEP = {2 + 2 * k: k for k in range(KD)}
    with ExitStack() as ctx:
        sb = lambda n, s, d=F32: ctx.enter_context(nc.sbuf_tensor(n + "_sb", s, d))
        sem = lambda n: ctx.enter_context(nc.semaphore(n))
        a_hi = sb("act_hi", [P, MF, T], F32R)
        a_lo = sb("act_lo", [P, MF, T], F32R)
        h = sb("h", [P, NT, D])
        stage = sb("stage", [P, 2, D])
        ms_now = sb("mix_mean_sq", [P, 12])
        gf = sb("final_rows", [P, D])
        rs_now = sb("rs_now", [P, 12])
        msq = sb("h_mean_sq", [P, NT])
        ms = sb("h_ms", [P, NT])
        rstd = sb("h_rstd", [P, NT])
        bank = ctx.enter_context(nc.psum_tensor("fin_bank", [P, 8, 512], F32))
        w_hi, w_lo, v_hi, v_lo, mx, squares = feed.w_hi, feed.w_lo, feed.v_hi, feed.v_lo, feed.mx, feed.squares
        w_lo_made, w_used, m_lo_made, m_used = feed.w_lo_made, feed.w_used, feed.m_lo_made, feed.m_used
        g2 = squares[:, 0:2, :].rearrange("p a n -> p (a n)")

        gf_landed = sem("gf_landed")
        h_landed = [sem(f"h_landed{i}") for i in range(NT)]
        g2_landed = sem("g2_landed")
        stat_done, ms_made, rs_made = sem("stat_done"), sem("mix_ms_made"), sem("mix_rs_made")
        proj_done, proj_read = sem("proj_done"), sem("proj_read")
        squared, rstd_step, rstd_made = sem("h_squared"), sem("h_rstd_step"), sem("h_rstd_made")
        v_made, transposed = sem("v_made"), sem("v_transposed")
        v_hi_made, v_lo_made = sem("v_hi_made"), sem("v_lo_made")
        silu_made, glu_made = sem("silu_made"), sem("glu_made")
        a_hi_made, a_lo_made = sem("a_hi_made"), sem("a_lo_made")
        down_done, down_read, y_made = sem("down_done"), sem("down_read"), sem("y_made")
        y_stored = [sem(f"y_stored{i}") for i in range(2)]
        block = ctx.enter_context(nc.Block())

        def blocks(eng, body):
            with eng.Fori(0, NBLK - 1) as b:
                body(b, True)
            body(NBLK - 1, False)

        def stream(b, q, more, split):
            if q + RING < PER:
                split(b, q + RING, (q + RING) % RING)
            elif more:
                n = START[q + RING - PER]
                split(b + 1, n, n)

        @block.sync
        def _(sp):
            sp.dma_start(gf[:, :], c["final_rows"]).then_inc(gf_landed, 16)
            panel = lambda b, q, s: feed.load_panel(sp, b, q, s)

            def h_load(b, t):
                sp.dma_start(h[:, t, :], c["x"][bass.ds(first_token(b) + P * t, P), :]).then_inc(h_landed[t], 16)

            def body(b, more):
                sp.wait_ge(stat_done, b + 1)
                sp.dma_start(g2, c["norm2_rows"]).then_inc(g2_landed, 16)
                for q in range(RING, KD):
                    stream(b, q, more, panel)
                with sp.Fori(0, MF // 2) as i:
                    for s in range(RING):
                        panel(b, RING * i + G0 + RING + s, s)
                sp.wait_ge(feed.f_stored, 32 * NCH)
                sp.wait_ge(feed.f_last_stored, 32)
                for q in range(D0, PER):
                    stream(b, q, more, panel)
                    if more and q - D0 in MIX_STEP:
                        feed.load_mix(sp, b + 1, MIX_STEP[q - D0])
                if more:
                    for q in START[:3]:
                        stream(b + 1, q, more, panel)
                for t in range(NT):
                    if more and t == 2:
                        stream(b + 1, START[3], more, panel)
                    sp.wait_ge(y_made, NT * b + t + 1)
                    sp.dma_start(c["out"][bass.ds(first_token(b) + P * t, P), :], stage[:, t % 2, :])\
                        .then_inc(y_stored[t % 2], 16)
                    if more:
                        h_load(b + 1, t)

            for s in y_stored:
                sp.nop().then_inc(s, 16)
            for t in range(NT):
                h_load(0, t)
            blocks(sp, body)
            for s in y_stored:
                sp.wait_ge(s, 16 * (1 + 2 * NBLK))

        @block.gpsimd
        def _(pool):
            def group_rstd(b):
                pool.wait_ge(ms_made, b + 1)
                pool.tensor_tensor(rs_now[:, :], ms_now[:, :], half[:, 0:12], ALU.pow).then_inc(rs_made, 1)

            def tile_rstd(b, n):
                t = n % NT
                pool.wait_ge(squared, 2 * NT * b + n + 1)
                pool.tensor_tensor(ms[:, t:t + 1], msq[:, t:t + 1], eps[:, :], ALU.add).then_inc(rstd_step, 1)
                pool.wait_ge(rstd_step, 2 * NT * b + n + 1)
                pool.tensor_tensor(rstd[:, t:t + 1], ms[:, t:t + 1], half[:, 0:1], ALU.pow).then_inc(rstd_made, 1)

            def body(b, more):
                for t in range(NT):
                    tile_rstd(b, t)
                if more:
                    for k in range(KD):
                        if k == 0:
                            pool.wait_ge(v_made, NT * b + NT)
                        feed.square_mix(pool, b + 1, k)
                for t in range(NT):
                    tile_rstd(b, NT + t)
                if more:
                    group_rstd(b + 1)

            group_rstd(0)
            blocks(pool, body)

        @block.scalar
        def _(act):
            split = lambda b, q, s, turn=None: feed.split_panel_hi(act, b, q, s, turn)

            def square(b, n):
                t = n % NT
                if n:
                    act.wait_ge(squared, 2 * NT * b + n)
                act.activation(mx.rearrange("p s n -> p (s n)"), h[:, t, :], ACT.Square, scale=D ** -0.5,
                               accum_out=msq[:, t:t + 1]).then_inc(squared, 1)

            def v_split(b, t):
                for g in range(2):
                    act.wait_ge(transposed, 2 * NT * b + 2 * t + g + 1)
                    act.activation(v_hi[:, 4 * g:4 * g + 4, P * t:P * t + P],
                                   bank[:, BANKS[2 * t + g], :].rearrange("p (k n) -> p k n", k=4), ACT.Copy)\
                        .then_inc(v_hi_made, 1)

            def body(b, more):
                for q in range(KD - 3):
                    stream(b, q, more, split)
                for t in range(NT):
                    act.wait_ge(proj_read, 24 * b + 16 + 2 * t + 2)
                    square(b, t)
                for t in range(NT):
                    v_split(b, t)
                for q in range(KD - 3, KD):
                    stream(b, q, more, split)
                with act.Fori(0, MF // 2) as i:
                    for p in range(2):
                        act.wait_ge(w_used, PER * b + RING * i + 2 * p + G0 + 1 + RING)
                        act.wait_ge(a_lo_made, MF * b + 2 * i + p + 1)
                        act.activation(stage[:, p, 0:T], bank[:, 2 * p, :], ACT.Silu).then_inc(silu_made, 1)
                        for s in (2 * p, 2 * p + 1):
                            split(b, RING * i + G0 + RING + s, s, i + G0 // RING + 1)
                        act.wait_ge(glu_made, MF * b + 2 * i + p + 3)
                        act.activation(a_hi[:, bass.ds(2 * i + p, 1), :].rearrange("p a n -> p (a n)"),
                                       stage[:, p, 0:T], ACT.Copy).then_inc(a_hi_made, 1)
                for q in range(D0, PER - 1):
                    stream(b, q, more, split)
                    if more and q - D0 in MIX_STEP:
                        feed.split_mix_hi(act, b + 1, MIX_STEP[q - D0])
                for t in range(NT):
                    act.wait_ge(down_read, 8 * b + 8 + 2 * t + 2)
                    if t == 0 and more:
                        act.wait_ge(m_used, KD * b + 2 * KD + 2)
                    square(b, NT + t)
                    if t == 1:
                        stream(b, PER - 1, more, split)

            blocks(act, body)

        @block.vector
        def _(dve):
            dve.nop().then_inc(glu_made, 2)
            dve.nop().then_inc(a_lo_made, 2)
            dve.nop().then_inc(down_read, 8)

            split = lambda b, q, s: feed.split_panel_lo(dve, b, q, s)

            def proj_add(b, g, j):
                t, n = j // 2, j % 2
                if j < 7:
                    dve.wait_ge(proj_done, 21 * b + 7 * g + j + 1)
                else:
                    dve.wait_ge(w_used, PER * b + LAST[g] + 1 + RING)
                part = h[:, t, 512 * n:512 * n + 512]
                if g == 0:
                    dve.wait_ge(h_landed[t], 16 * b + 16)
                else:
                    dve.wait_ge(proj_read, 24 * b + 8 * g - 8 + j + 1)
                dve.scalar_tensor_tensor(out=part, in0=bank[:, BANKS[j], :], scalar=rs_now[:, 4 * g + t:4 * g + t + 1],
                                         in1=part, op0=ALU.mult, op1=ALU.add).then_inc(proj_read, 1)

            def v_norm(b, t):
                dve.wait_ge(rstd_made, 2 * NT * b + t + 1)
                if t < 2:
                    dve.wait_ge(y_stored[t], 16 * (2 * b + 1))
                else:
                    dve.wait_ge(transposed, 2 * NT * b + 2 * t - 2)
                if t == 0:
                    dve.wait_ge(g2_landed, 16 * b + 16)
                dve.scalar_tensor_tensor(out=stage[:, t % 2, :], in0=h[:, t, :], scalar=rstd[:, t:t + 1], in1=g2,
                                         op0=ALU.mult, op1=ALU.mult).then_inc(v_made, 1)

            def v_split(b, t):
                for g in range(2):
                    dve.wait_ge(v_hi_made, 2 * NT * b + 2 * t + g + 1)
                    part = lambda v: v[:, 4 * g:4 * g + 4, P * t:P * t + P]
                    dve.tensor_tensor(part(v_lo), bank[:, BANKS[2 * t + g], :].rearrange("p (k n) -> p k n", k=4),
                                      part(v_hi).bitcast(F32), ALU.subtract).then_inc(v_lo_made, 1)

            def mix_means(b):
                dve.wait_ge(stat_done, b + 1)
                dve.tensor_scalar(ms_now[:, :], bank[:, BANKS[0], 0:12], EPS, None, ALU.add).then_inc(ms_made, 1)

            def y_norm(b, t):
                if t == 0:
                    dve.wait_ge(gf_landed, 16)
                dve.wait_ge(rstd_made, 2 * NT * b + NT + t + 1)
                if t >= 2:
                    dve.wait_ge(y_stored[t % 2], 16 * (2 * b + 2))
                dve.scalar_tensor_tensor(out=stage[:, t % 2, :], in0=h[:, t, :], scalar=rstd[:, t:t + 1],
                                         in1=gf[:, :], op0=ALU.mult, op1=ALU.mult).then_inc(y_made, 1)

            def body(b, more):
                dve.wait_ge(rs_made, b + 1)
                for q in range(KD - 2):
                    if q in LAST[:2]:
                        for j in range(8):
                            proj_add(b, GROUP_OF[q], j)
                    if q < KD - 3:
                        stream(b, q, more, split)
                proj_tile = lambda t: [proj_add(b, 2, j) for j in (2 * t, 2 * t + 1)]
                proj_tile(0)
                proj_tile(1)
                v_norm(b, 0)
                proj_tile(2)
                v_norm(b, 1)
                proj_tile(3)
                v_norm(b, 2)
                v_split(b, 0)
                v_norm(b, 3)
                v_split(b, 1)
                v_split(b, 2)
                v_split(b, 3)
                for q in range(KD - 3, KD):
                    stream(b, q, more, split)
                with dve.Fori(0, MF // 2) as i:
                    for p in range(2):
                        m = 2 * i + p
                        split(b, RING * i + G0 + RING + 2 * p, 2 * p)
                        dve.wait_ge(silu_made, MF * b + m + 1)
                        dve.wait_ge(w_used, PER * b + RING * i + 2 * p + G0 + 2 + RING)
                        dve.tensor_tensor(stage[:, p, 0:T], bank[:, 2 * p + 1, :], stage[:, p, 0:T], ALU.mult)\
                            .then_inc(glu_made, 1)
                        split(b, RING * i + G0 + RING + 2 * p + 1, 2 * p + 1)
                        dve.wait_ge(a_hi_made, MF * b + m + 1)
                        at = lambda a: a[:, bass.ds(m, 1), :].rearrange("p a n -> p (a n)")
                        dve.tensor_tensor(at(a_lo), stage[:, p, 0:T], at(a_hi).bitcast(F32), ALU.subtract)\
                            .then_inc(a_lo_made, 1)
                for q in range(D0, PER - 1):
                    stream(b, q, more, split)
                    if more and q - D0 in MIX_STEP:
                        feed.split_mix_lo(dve, b + 1, MIX_STEP[q - D0])
                for t in range(NT):
                    for j in (2 * t, 2 * t + 1):
                        if j < 7:
                            dve.wait_ge(down_done, 7 * b + j + 1)
                        else:
                            dve.wait_ge(w_used, PER * b + PER + RING)
                        part = h[:, t, 512 * (j % 2):512 * (j % 2) + 512]
                        dve.tensor_tensor(part, bank[:, BANKS[j], :], part, ALU.add).then_inc(down_read, 1)
                    if t == 2 and more:
                        mix_means(b + 1)
                    if t and not more:
                        y_norm(b, t - 1)
                if more:
                    y_norm(b, 0)
                    stream(b, PER - 1, more, split)
                    y_norm(b, 1)
                    y_norm(b, 2)
                y_norm(b, NT - 1)

            mix_means(0)
            blocks(dve, body)

        @block.tensor
        def _(pe):
            pe.wait_ge(feed.g_landed, 32)

            def product(b, q, src, k, j, first, last):
                t, n, s = j // 2, j % 2, q % RING
                return split_product(pe, bank[:, BANKS[j], :], [x[:, k, P * t:P * t + P] for x in src],
                                     [w[:, s, 512 * n:512 * n + 512] for w in (w_hi, w_lo)], first, last)

            def statistics(b):
                pe.wait_ge(down_read, 8 * b + 1)
                pe.wait_ge(m_used, KD * b + KD + 2)
                for g in range(3):
                    for t in range(NT):
                        ins = pe.matmul(bank[:, BANKS[0], 4 * g + t:4 * g + t + 1], squares[:, g, P * t:P * t + P],
                                        feed.group_means[:, g:g + 1], start=(g == 0 and t == 0), stop=True,
                                        skip_group_check=True)
                ins.then_inc(stat_done, 1)

            def transpose(b, t):
                pe.wait_ge(v_made, NT * b + t + 1)
                for g in range(2):
                    for k in range(4):
                        ins = pe.transpose(bank[:, BANKS[2 * t + g], P * k:P * k + P],
                                           stage[:, t % 2, (4 * g + k) * P:(4 * g + k + 1) * P], ident[:, :])
                    ins.then_inc(transposed, 1)

            def body(b, more):
                statistics(b)
                for k in range(KD - 2):
                    g = GROUP_OF[k]
                    pe.wait_ge(m_lo_made, KD * b + k + 3)
                    pe.wait_ge(w_lo_made, PER * b + (max(START.index(k), k) if k < RING else k) + 1 + RING)
                    for j in FIRST_TURN if k == 0 else range(8):
                        if k == 0:
                            pe.wait_ge(down_read, 8 * b + j + 1)
                            if j == 0:
                                pe.wait_ge(ms_made, b + 1)
                        elif k in FIRST:
                            pe.wait_ge(proj_read, 24 * b + 8 * g - 8 + j + 1)
                        ins = product(b, k, (v_hi, v_lo), k, j, k in FIRST, k in LAST)
                        if k in LAST and j < 7:
                            ins.then_inc(proj_done, 1)
                    ins.then_inc(w_used, 1)
                pe.wait_ge(m_lo_made, KD * b + KD + 2)
                pe.wait_ge(w_lo_made, PER * b + KD + RING)
                for j in range(8):
                    pe.wait_ge(proj_read, 24 * b + 8 + j + 1)
                    for k in (KD - 2, KD - 1):
                        ins = product(b, k, (v_hi, v_lo), k, j, k == KD - 2, k == KD - 1)
                        if j == 7:
                            ins.then_inc(w_used, 1)
                    if j < 7:
                        ins.then_inc(proj_done, 1)
                for t in range(NT):
                    transpose(b, t)
                with pe.Fori(0, MF // 2) as i:
                    pe.wait_ge(v_lo_made, 2 * NT * (b + 1))
                    for p in range(2):
                        pe.wait_ge(glu_made, MF * b + 2 * i + p + 1)
                        for s in (2 * p, 2 * p + 1):
                            pe.wait_ge(w_lo_made, PER * b + RING * i + G0 + s + 1 + RING)
                            for k in range(KD):
                                ins = split_product(pe, bank[:, s, :],
                                                    [w[:, s, P * k:P * k + P] for w in (w_hi, w_lo)],
                                                    (v_hi[:, k, :], v_lo[:, k, :]), k == 0, k == KD - 1)
                            ins.then_inc(w_used, 1)
                for k in range(MF):
                    pe.wait_ge(a_lo_made, MF * b + k + 3)
                    pe.wait_ge(w_lo_made, PER * b + D0 + k + 1 + RING)
                    for j in range(8):
                        if k == 0 and BANKS[j] < 4:
                            pe.wait_ge(glu_made, MF * b + MF + 1 + BANKS[j] // 2)
                        ins = product(b, D0 + k, (a_hi, a_lo), k, j, k == 0, k == MF - 1)
                        if k == MF - 1 and j < 7:
                            ins.then_inc(down_done, 1)
                    ins.then_inc(w_used, 1)

            blocks(pe, body)


def build(nc, c):
    with ExitStack() as ctx:
        ident = ctx.enter_context(nc.sbuf_tensor("ident_sb", [P, P], F32))
        half = ctx.enter_context(nc.sbuf_tensor("minus_half_sb", [P, 12], F32))
        eps = ctx.enter_context(nc.sbuf_tensor("eps_sb", [P, 1], F32))
        tail = ctx.enter_context(nc.sbuf_tensor("mix_tails_sb", [P, 6, HALO], F32))
        tail_stored = ctx.enter_context(nc.semaphore("tail_stored"))
        project(nc, c, ident, half, eps, tail, tail_stored)
        feed = Feed(nc, ctx, c)
        fourier(nc, c, feed, tail_stored)
        finish(nc, c, feed, ident, half, eps)


def dft_tables(length, rows, freqs):
    turns = (rows[:, None] * freqs[None, :]) % length * (2 * np.pi / length)
    return (np.stack([np.cos(turns), np.sin(turns)], axis=1) / np.sqrt(length)).astype(np.float32)


def constants():
    k = {"ident": np.eye(P, dtype=np.float32), "reversal": np.eye(P, dtype=np.float32)[::-1].copy(),
         "minus_half": np.full((P, 12), -0.5, np.float32),
         "group_means": np.tile(np.float32([1 / CONV, 1 / CONV, 1 / FOUR]), (P, 1)), "eps": np.full((P, 1), EPS, np.float32)}
    back = np.arange(8)[::-1]
    counts = np.stack([np.minimum(w - 1 - w // 2, back) + w // 2 + 1 for w in WINDOWS])
    k["inv_counts"] = np.tile(np.repeat(1.0 / counts, 32, axis=0)[:, None, :], (1, 3, 1)).astype(np.float32)
    dims = np.arange(HD)
    head = dft_tables(HD, dims, dims)
    tables = np.zeros((P, 2, P), np.float32)
    for n in range(P // HD):
        tables[HD * n:HD * n + HD, :, HD * n:HD * n + HD] = head
    k["head_tables"] = tables
    for name, length, freqs, chunks in (("table1", L1, NCH * KCH, NCH), ("table2", L2, K2, 1)):
        at, width = np.arange(1, length // 2 + 1), freqs // chunks
        full = len(at) // P * P
        out = np.zeros((chunks, full // P + 1, P, 2 * width), np.float32)
        for n in range(chunks):
            f = np.arange(1 + n * width, 1 + (n + 1) * width)
            out[n, :-1] = dft_tables(length, at[:full], f).reshape(-1, P, 2 * width)
            last = np.append(at[full:], 0)
            out[n, -1, 0:len(last)] = dft_tables(length, last, f).reshape(len(last), 2 * width)
        k[name] = out if chunks > 1 else out[0]
    return k


def kernel(x_prompt, x_sample, meta_tokens, norm1_g, w_in, conv_w, pool_w, pool_scale, mix_g, w_out, norm2_g,
           w_gate_up, w_down, final_g):
    import concourse.bacc as bacc
    from concourse.bass_utils import run_bass_kernel_spmd

    asc = np.ascontiguousarray
    x_prompt, x_sample, w_in, w_out, w_gu, w_down = (
        np.asarray(a) for a in (x_prompt, x_sample, w_in[0], w_out[0], w_gate_up[0], w_down[0]))
    arrays = constants()
    arrays["x"] = np.concatenate([x_prompt[0], x_sample[0]])
    arrays["meta"] = np.asarray(meta_tokens)
    for name, g in (("norm1_rows", norm1_g[0]), ("norm2_rows", norm2_g[0]), ("final_rows", final_g)):
        arrays[name] = asc(np.broadcast_to(np.asarray(g), (P, D)))

    def column_panels(w):
        return asc(w.reshape(KD, P, -1, P).transpose(2, 1, 0, 3)).reshape(-1, P, D)

    four = column_panels(w_in[:, 3 * CONV + CONV:])
    arrays["w_in_panels"] = np.concatenate([column_panels(w_in[:, 0:3 * CONV]), four])
    arrays["w_pool_T"] = asc(w_in[:, 3 * CONV:4 * CONV].T).reshape(4, GROUP, D)
    arrays["pool_w"] = asc(np.asarray(pool_w[0]))
    arrays["conv_cols"] = asc(np.asarray(conv_w[0]).reshape(3, 3, P).transpose(2, 1, 0))

    def pool_order(a):
        return a.reshape(4, 3, 32, -1).transpose(1, 0, 2, 3).reshape(CONV, -1)

    def mixed(a):
        a = np.asarray(a).reshape(D, -1)
        return np.concatenate([a[0:CONV], pool_order(a[CONV:2 * CONV]), a[2 * CONV:]])

    arrays["pool_scale_cols"] = asc(pool_order(np.asarray(pool_scale[0])).reshape(3, P).T)
    arrays["mix_g_cols"] = asc(mixed(mix_g[0]).reshape(KD, P).T)
    gate, up = column_panels(w_gu[:, 0:DFF]), column_panels(w_gu[:, DFF:])
    arrays["w_panels"] = np.concatenate([mixed(w_out).reshape(KD, P, D),
                                         np.stack([gate, up], axis=1).reshape(-1, P, D),
                                         w_down.reshape(MF, P, D)])

    nc = bacc.Bacc("TRN2", target_bir_lowering=False, num_devices=1)
    c = {n: nc.dram_tensor(n, list(a.shape), F32, kind="ExternalInput").ap() for n, a in arrays.items()}
    c["mixT"] = nc.dram_tensor("mixT", [D, META + SEQ + DEC], F32).ap()
    c["xf"] = nc.dram_tensor("xf", [L1 + L2, FOUR], F32).ap()
    c["out"] = nc.dram_tensor("out", [SEQ + DEC, D], F32, kind="ExternalOutput").ap()
    build(nc, c)
    r = run_bass_kernel_spmd(nc, [arrays], core_ids=[0])
    out = r.results[0]["out"]
    return out[None, 0:SEQ], out[None, SEQ:]
```
